# Optimizing a Trainium2 kernel written in Bass

```python
import math
import jax
import jax.numpy as jnp
from jax import lax
import numpy as np

D_MODEL = 1024
BATCH = 1
SEQ = 128
DEPTH = 2
DEC_BATCH = 1
DEC_SEQ = 512
PAST_LEN = 128

GRID_W = 64
NA_HEADS = 8
NA_HEAD_DIM = 64
NA_WIN_H = 8
NA_WIN_W = 16
ML_HEADS = 4
ML_HEAD_DIM = 128
ML_CHUNK = 128
CONV_WIDTH = 3
D_FF = 2816
N_MOD = 9
EPS = 1e-6
ATTN_QBLOCK = 128
N_AB = (DEPTH + 1) // 2
N_C = DEPTH // 2
NA_WIDTH = NA_HEADS * NA_HEAD_DIM
ML_WIDTH = ML_HEADS * ML_HEAD_DIM
AB_IN = 3 * NA_WIDTH + 4 * ML_WIDTH + 4 * ML_HEADS
AB_OUT = NA_WIDTH + ML_WIDTH
AB_SPLITS = (NA_WIDTH, 2 * NA_WIDTH, 3 * NA_WIDTH, 3 * NA_WIDTH + ML_WIDTH, 3 * NA_WIDTH + 2 * ML_WIDTH, 3 * NA_WIDTH + 3 * ML_WIDTH, 3 * NA_WIDTH + 4 * ML_WIDTH)
SC_WIDTH = D_MODEL

kernel_name = 'hybrid_dit_natten_mlstm_shortconv_step'

def rmsnorm(x, g):
    xf = x.astype(jnp.float32)
    y = xf * lax.rsqrt(jnp.mean(xf * xf, axis=-1, keepdims=True) + EPS)
    return (y * g.astype(jnp.float32)).astype(x.dtype)

def modulation(cond, w, b):
    m = jax.nn.silu(cond) @ w + b
    return m.reshape(cond.shape[0], 1, N_MOD, D_MODEL)

def modulate_in(x, g_pre, mod, j):
    return rmsnorm(x, g_pre) * (1.0 + mod[:, :, 3 * j + 1]) + mod[:, :, 3 * j]

def gated_residual(x, out, g_post, mod, j, weight):
    return x + weight * mod[:, :, 3 * j + 2] * rmsnorm(out, g_post)

def swiglu(h, w13, w2):
    a, g = jnp.split(h @ w13, 2, axis=-1)
    return (jax.nn.silu(g) * a) @ w2

def ffn_sublayer(x, mod, j, g_pre, g_post, w13, w2):
    h = modulate_in(x, g_pre, mod, j)
    return gated_residual(x, swiglu(h, w13, w2), g_post, mod, j, 0.5)

def split_heads(t, n_heads, head_dim):
    B, L, _ = t.shape
    return t.reshape(B, L, n_heads, head_dim).transpose(0, 2, 1, 3)

def merge_heads(t):
    B, H, L, dh = t.shape
    return t.transpose(0, 2, 1, 3).reshape(B, L, H * dh)

def dwconv_centred(u, w, b):
    L = u.shape[1]
    pad = CONV_WIDTH // 2
    up = jnp.pad(u, ((0, 0), (pad, pad), (0, 0)))
    y = b
    for i in range(CONV_WIDTH):
        y = y + up[:, i:i + L] * w[i]
    return y

def shortconv_mixer(h, w_in, conv_w, conv_b, w_out):
    gb, gc, xin = jnp.split(h @ w_in, 3, axis=-1)
    return (gb * dwconv_centred(gc * xin, conv_w, conv_b)) @ w_out

def context_attention(q, k, v):
    B, H, Lc, dh = q.shape
    nb = Lc // ATTN_QBLOCK
    scale = dh ** -0.5
    qb = jnp.moveaxis(q.reshape(B, H, nb, ATTN_QBLOCK, dh), 2, 0)

    def block(qblk):
        s = jnp.einsum('bhqd,bhkd->bhqk', qblk, k).astype(jnp.float32) * scale
        p = jax.nn.softmax(s, axis=-1).astype(v.dtype)
        return jnp.einsum('bhqk,bhkd->bhqd', p, v)

    o = lax.map(block, qb)
    return jnp.moveaxis(o, 0, 2).reshape(B, H, Lc, dh)

def na_latent(q, k, v, k_ctx, v_ctx, rpb):
    B, L, _ = q.shape
    R = L // GRID_W
    kh = min(NA_WIN_H, R)
    scale = NA_HEAD_DIM ** -0.5
    grid = lambda t: t.reshape(B, R, GRID_W, NA_HEADS, NA_HEAD_DIM).transpose(0, 3, 1, 2, 4)
    qg, kg, vg = grid(q), grid(k), grid(v)
    rows = jnp.arange(R)
    cols = jnp.arange(GRID_W)
    rs = jnp.clip(rows - kh // 2, 0, R - kh)
    cs = jnp.clip(cols - NA_WIN_W // 2, 0, GRID_W - NA_WIN_W)
    row_idx = rs[:, None] + jnp.arange(kh)[None, :]
    k_rows = kg[:, :, row_idx]
    v_rows = vg[:, :, row_idx]
    s_loc = jnp.einsum('bhrcd,bhrjwd->bhrcjw', qg, k_rows).astype(jnp.float32) * scale
    col_in = (cols[None, :] >= cs[:, None]) & (cols[None, :] < cs[:, None] + NA_WIN_W)
    dr = row_idx - rows[:, None] + (NA_WIN_H - 1)
    dc = jnp.clip(cols[None, :] - cols[:, None], -(NA_WIN_W - 1), NA_WIN_W - 1) + (NA_WIN_W - 1)
    bias = rpb[:, dr[:, None, :, None], dc[None, :, None, :]].astype(jnp.float32)
    s_loc = jnp.where(col_in[None, None, None, :, None, :], s_loc + bias[None], -jnp.inf)
    s_ctx = jnp.einsum('bhrcd,bhsd->bhrcs', qg, k_ctx).astype(jnp.float32) * scale
    n_loc = kh * GRID_W
    s_all = jnp.concatenate([s_loc.reshape(B, NA_HEADS, R, GRID_W, n_loc), s_ctx], axis=-1)
    p = jax.nn.softmax(s_all, axis=-1).astype(v.dtype)
    p_loc = p[..., :n_loc].reshape(B, NA_HEADS, R, GRID_W, kh, GRID_W)
    p_ctx = p[..., n_loc:]
    out = jnp.einsum('bhrcjw,bhrjwd->bhrcd', p_loc, v_rows) + jnp.einsum('bhrcs,bhsd->bhrcd', p_ctx, v_ctx)
    return out.transpose(0, 2, 3, 1, 4).reshape(B, L, NA_WIDTH)

def mlstm_scan(q, k, v, log_i, log_f, C0, n0, m0):
    B, H, L, dh = q.shape
    nc = L // ML_CHUNK
    chunks = lambda t: jnp.moveaxis(t.reshape((B, H, nc, ML_CHUNK) + t.shape[3:]), 2, 0)
    tril = jnp.tril(jnp.ones((ML_CHUNK, ML_CHUNK), dtype=bool))

    def step(carry, inp):
        C, n, m = carry
        qb, kb, vb, ib, fb = inp
        bcum = jnp.cumsum(fb, axis=-1)
        a = bcum + m[..., None]
        Dm = jnp.where(tril, bcum[..., :, None] - bcum[..., None, :] + ib[..., None, :], -jnp.inf)
        m_t = jnp.maximum(a, jnp.max(Dm, axis=-1))
        w_inter = jnp.exp(a - m_t)
        Wd = jnp.exp(Dm - m_t[..., None])
        s = jnp.einsum('bhtd,bhsd->bhts', qb, kb) * Wd
        num = w_inter[..., None] * jnp.einsum('bhtd,bhde->bhte', qb, C) + jnp.einsum('bhts,bhse->bhte', s, vb)
        den = w_inter * jnp.einsum('bhtd,bhd->bht', qb, n) + jnp.sum(s, axis=-1)
        h = num / jnp.maximum(jnp.abs(den), jnp.exp(-m_t))[..., None]
        w_last = Wd[..., -1, :]
        wi_last = w_inter[..., -1]
        C_new = wi_last[..., None, None] * C + jnp.einsum('bhs,bhsd,bhse->bhde', w_last, kb, vb)
        n_new = wi_last[..., None] * n + jnp.einsum('bhs,bhsd->bhd', w_last, kb)
        return (C_new, n_new, m_t[..., -1]), h

    (C, n, m), hs = lax.scan(step, (C0, n0, m0), (chunks(q), chunks(k), chunks(v), chunks(log_i), chunks(log_f)))
    h = jnp.moveaxis(hs, 0, 2).reshape(B, H, L, dh)
    return h, C, n, m

def mlstm_mixer(q, k, v, o, gates, gate_b, hnorm, C0, n0, m0):
    B, L, _ = q.shape
    dt = q.dtype
    f32 = jnp.float32
    qh = split_heads(q.astype(f32), ML_HEADS, ML_HEAD_DIM)
    kh = split_heads(k.astype(f32), ML_HEADS, ML_HEAD_DIM) * (ML_HEAD_DIM ** -0.5)
    vh = split_heads(v.astype(f32), ML_HEADS, ML_HEAD_DIM)
    g = (gates.astype(f32).reshape(B, L, 4, ML_HEADS) + gate_b.astype(f32)).transpose(2, 0, 3, 1)
    C0, n0, m0 = C0.astype(f32), n0.astype(f32), m0.astype(f32)
    h_f, Cf, nf, mf = mlstm_scan(qh, kh, vh, g[0], jax.nn.log_sigmoid(g[1]), C0[:, 0], n0[:, 0], m0[:, 0])
    flip = lambda t: jnp.flip(t, axis=2)
    h_b, Cb, nb, mb = mlstm_scan(flip(qh), flip(kh), flip(vh), flip(g[2]), flip(jax.nn.log_sigmoid(g[3])), C0[:, 1], n0[:, 1], m0[:, 1])
    h = (h_f + flip(h_b)).transpose(0, 2, 1, 3)
    h = rmsnorm(h, hnorm.reshape(ML_HEADS, ML_HEAD_DIM)).reshape(B, L, ML_WIDTH)
    out = (jax.nn.sigmoid(o.astype(f32)) * h).astype(dt)
    return out, jnp.stack([Cf, Cb], axis=1), jnp.stack([nf, nb], axis=1), jnp.stack([mf, mb], axis=1)

def ab_mixer_context(h, w_in, w_out, gate_b, hnorm):
    B = h.shape[0]
    qa, ka, va, qm, km, vm, om, gates = jnp.split(h @ w_in, AB_SPLITS, axis=-1)
    k_h = split_heads(ka, NA_HEADS, NA_HEAD_DIM)
    v_h = split_heads(va, NA_HEADS, NA_HEAD_DIM)
    a_out = merge_heads(context_attention(split_heads(qa, NA_HEADS, NA_HEAD_DIM), k_h, v_h))
    C0 = jnp.zeros((B, 2, ML_HEADS, ML_HEAD_DIM, ML_HEAD_DIM), jnp.float32)
    n0 = jnp.zeros((B, 2, ML_HEADS, ML_HEAD_DIM), jnp.float32)
    m0 = jnp.zeros((B, 2, ML_HEADS), jnp.float32)
    m_out, C, n, m = mlstm_mixer(qm, km, vm, om, gates, gate_b, hnorm, C0, n0, m0)
    out = jnp.concatenate([a_out, m_out], axis=-1) @ w_out
    return out, k_h, v_h, C, n, m

def ab_mixer_latent(h, k_ctx, v_ctx, C0, n0, m0, w_in, w_out, rpb, gate_b, hnorm):
    qa, ka, va, qm, km, vm, om, gates = jnp.split(h @ w_in, AB_SPLITS, axis=-1)
    a_out = na_latent(qa, ka, va, k_ctx, v_ctx, rpb)
    m_out, _, _, _ = mlstm_mixer(qm, km, vm, om, gates, gate_b, hnorm, C0, n0, m0)
    return jnp.concatenate([a_out, m_out], axis=-1) @ w_out

def setup_inputs(seed: int = 0) -> dict:
    key = jax.random.key(seed)
    ks = jax.random.split(key, 24)
    f32 = jnp.float32
    D = D_MODEL
    nrm = lambda k, shape, s: jax.random.normal(k, shape, f32) * s
    ig_b = nrm(ks[17], (N_AB, 2, 1, ML_HEADS), 0.1)
    fg_b = 3.0 + 3.0 * jax.random.uniform(ks[18], (N_AB, 2, 1, ML_HEADS), f32)
    return {
        'x_prompt': nrm(ks[0], (BATCH, SEQ, D), 1.0),
        'x_sample': nrm(ks[1], (DEC_BATCH, DEC_SEQ, D), 1.0),
        'cache_k': nrm(ks[2], (DEC_BATCH, N_AB, NA_HEADS, PAST_LEN, NA_HEAD_DIM), 1.0),
        'cache_v': nrm(ks[3], (DEC_BATCH, N_AB, NA_HEADS, PAST_LEN, NA_HEAD_DIM), 1.0),
        'state_C': nrm(ks[4], (DEC_BATCH, N_AB, 2, ML_HEADS, ML_HEAD_DIM, ML_HEAD_DIM), 0.3),
        'state_n': nrm(ks[5], (DEC_BATCH, N_AB, 2, ML_HEADS, ML_HEAD_DIM), 0.3),
        'state_m': nrm(ks[6], (DEC_BATCH, N_AB, 2, ML_HEADS), 1.0),
        'c': nrm(ks[7], (DEC_BATCH, D), 1.0),
        'c_ctx': nrm(ks[8], (D,), 1.0),
        'ada_w': nrm(ks[9], (DEPTH, D, N_MOD * D), 0.5 * D ** -0.5),
        'ada_b': nrm(ks[10], (DEPTH, N_MOD * D), 0.1),
        'norm_g': 1.0 + nrm(ks[11], (DEPTH, 3, 2, D), 0.05),
        'ffn_w13': nrm(ks[12], (DEPTH, 2, D, 2 * D_FF), D ** -0.5),
        'ffn_w2': nrm(ks[13], (DEPTH, 2, D_FF, D), D_FF ** -0.5),
        'ab_w_in': nrm(ks[14], (N_AB, D, AB_IN), D ** -0.5),
        'ab_w_out': nrm(ks[15], (N_AB, AB_OUT, D), AB_OUT ** -0.5),
        'na_rpb': nrm(ks[16], (N_AB, NA_HEADS, 2 * NA_WIN_H - 1, 2 * NA_WIN_W - 1), 0.1),
        'ml_gate_b': jnp.concatenate([ig_b, fg_b], axis=2).reshape(N_AB, 4, ML_HEADS),
        'ml_hnorm': 1.0 + nrm(ks[19], (N_AB, ML_WIDTH), 0.05),
        'sc_w_in': nrm(ks[20], (N_C, D, 3 * SC_WIDTH), D ** -0.5),
        'sc_conv_w': nrm(ks[21], (N_C, CONV_WIDTH, SC_WIDTH), CONV_WIDTH ** -0.5),
        'sc_conv_b': nrm(ks[22], (N_C, SC_WIDTH), 0.02),
        'sc_w_out': nrm(ks[23], (N_C, SC_WIDTH, D), SC_WIDTH ** -0.5),
    }

def reference(x_prompt, x_sample, cache_k, cache_v, state_C, state_n, state_m, c, c_ctx,
              ada_w, ada_b, norm_g, ffn_w13, ffn_w2, ab_w_in, ab_w_out, na_rpb, ml_gate_b, ml_hnorm,
              sc_w_in, sc_conv_w, sc_conv_b, sc_w_out):
    y_p, y_s = x_prompt, x_sample
    new_k, new_v, new_C, new_n, new_m = [], [], [], [], []
    for l in range(DEPTH):
        mod_p = modulation(c_ctx[None, :], ada_w[l], ada_b[l])
        mod_s = modulation(c, ada_w[l], ada_b[l])
        g = norm_g[l]
        y_p = ffn_sublayer(y_p, mod_p, 0, g[0, 0], g[0, 1], ffn_w13[l, 0], ffn_w2[l, 0])
        y_s = ffn_sublayer(y_s, mod_s, 0, g[0, 0], g[0, 1], ffn_w13[l, 0], ffn_w2[l, 0])
        h_p = modulate_in(y_p, g[1, 0], mod_p, 1)
        h_s = modulate_in(y_s, g[1, 0], mod_s, 1)
        j = l // 2
        if l % 2 == 0:
            out_p, k_c, v_c, C_c, n_c, m_c = ab_mixer_context(h_p, ab_w_in[j], ab_w_out[j], ml_gate_b[j], ml_hnorm[j])
            new_k.append(k_c)
            new_v.append(v_c)
            new_C.append(C_c)
            new_n.append(n_c)
            new_m.append(m_c)
            out_s = ab_mixer_latent(h_s, cache_k[:, j], cache_v[:, j], state_C[:, j], state_n[:, j], state_m[:, j],
                                    ab_w_in[j], ab_w_out[j], na_rpb[j], ml_gate_b[j], ml_hnorm[j])
        else:
            out_p = shortconv_mixer(h_p, sc_w_in[j], sc_conv_w[j], sc_conv_b[j], sc_w_out[j])
            out_s = shortconv_mixer(h_s, sc_w_in[j], sc_conv_w[j], sc_conv_b[j], sc_w_out[j])
        y_p = gated_residual(y_p, out_p, g[1, 1], mod_p, 1, 1.0)
        y_s = gated_residual(y_s, out_s, g[1, 1], mod_s, 1, 1.0)
        y_p = ffn_sublayer(y_p, mod_p, 2, g[2, 0], g[2, 1], ffn_w13[l, 1], ffn_w2[l, 1])
        y_s = ffn_sublayer(y_s, mod_s, 2, g[2, 0], g[2, 1], ffn_w13[l, 1], ffn_w2[l, 1])
    new_cache_k = jnp.stack(new_k, axis=1)
    new_cache_v = jnp.stack(new_v, axis=1)
    new_state_C = jnp.stack(new_C, axis=1)
    new_state_n = jnp.stack(new_n, axis=1)
    new_state_m = jnp.stack(new_m, axis=1)
    return (y_p, y_s, new_cache_k, new_cache_v, new_state_C, new_state_n, new_state_m)


_drawn_inputs = setup_inputs


def setup_inputs(seed=0):
    import zlib

    import numpy as np

    out = dict(_drawn_inputs(seed))
    spreads = {}
    factors = {'na_rpb': 37.588, 'ml_hnorm': 15.331, 'sc_conv_b': 8.0, 'cache_k': 6.852, 'cache_v': 5.73}
    for name, (base, spread) in spreads.items():
        noise = np.random.default_rng([zlib.crc32(name.encode()), seed]).standard_normal(out[name].shape)
        drawn = base * np.exp(spread * noise) if base else spread * noise
        out[name] = jnp.asarray(drawn.astype(out[name].dtype))
    for name, factor in factors.items():
        out[name] = (out[name] * factor).astype(out[name].dtype)
    return out
```

```python
from contextlib import ExitStack, contextmanager

import concourse.bass as bass
from concourse import mybir

F32 = mybir.dt.float32
F32R = mybir.dt.float32r
ALU = mybir.AluOpType
ACT = mybir.ActivationFunctionType
AX = mybir.AxisListType
P = 128

D = 1024
LAT, CTX = 512, 128
TOK = LAT + CTX
NT = TOK // P
CT = LAT // P
KD = D // P
HT = TOK // 2
FF = 2816
HF = FF // P // 2
NMOD = 9 * D
MODW = 512
EPS = 1e-6
NAH, NAD = 8, 64
MLH, MLD = 4, 128
GRID_W, ROWS = 64, LAT // 64
WIN_H, WIN_W = 8, 16
DR, DC = 2 * WIN_H - 1, 2 * WIN_W - 1
PADW = 2 * GRID_W - 1
TJ = ROWS + 2 * (CT - 1)
BIG = 1e30
AB_IN = 3 * NAH * NAD + 4 * MLH * MLD + 4 * MLH
NG = 4 * MLH
SUBS = ["ffn", "ab", "ffn", "ffn", "sc", "ffn"]

FFN_IN, FFN_OUT = 2 * HF, 2 * HF
AB_UNITS = (AB_IN - NG) // P
AB_OUT = 2 * KD
SC_IN, SC_OUT = 3 * KD, 2 * KD
COUNT = {"ffn": 2 * (FFN_IN + FFN_OUT), "ab": AB_UNITS + 1 + AB_OUT, "sc": SC_IN + SC_OUT}
UB = [sum(COUNT[k] for k in SUBS[:s]) for s in range(len(SUBS) + 1)]


class Steps:

    def __init__(self, eng, sem):
        self.eng, self.sem, self.n, self.off = eng, sem, 0, 0

    def link(self, ins):
        self.n += 1
        ins.then_inc(self.sem, 1)
        self.eng.wait_ge(self.sem, self.n + self.off)

    @contextmanager
    def loop(self, start, end, per):
        n0 = self.n
        with self.eng.Fori(start, end) as i:
            self.off = (i - start) * per
            yield i
            assert self.n - n0 == per, (self.n - n0, per)
        self.n, self.off = n0 + per * (end - start), 0


def need(eng, sem, n):
    if not isinstance(n, int) or n > 0:
        eng.wait_ge(sem, n)


class Evacs:

    def __init__(self):
        self.n = [0, 0]

    def phase(self, base, units):
        start = list(self.n)
        for u in range(base, base + units):
            self.n[u % 2] += 1
        return start


def build(nc, x_prompt, x_sample, cache_k, cache_v, state_C, state_n, state_m, c, c_ctx, ada_w,
          ada_b, norm_g, ffn_w13, ffn_w2, ab_w_in, ab_w_out, na_rpb, ml_gate_b, ml_hnorm, sc_w_in,
          sc_conv_w, sc_conv_b, sc_w_out, k_ident, k_sel, k_mlmask, k_namask,
          y_prompt, y_sample, new_k, new_v, new_C, new_n, new_m):
    ctx = ExitStack()
    with ctx:
        sb = lambda name, shape, dt=F32: ctx.enter_context(nc.sbuf_tensor(name, shape, dt))
        sem = lambda name: ctx.enter_context(nc.semaphore(name))
        at = lambda name, shape, off, dt=F32: nc.alloc_sbuf_tensor_at(name, shape, dt, offset=off)

        base = nc.sbuf_base
        base = (base + 31) // 32 * 32
        end = nc.sbuf_usable_end
        o = base

        def take(name, shape, dt=F32):
            nonlocal o
            t = at(name, shape, o, dt)
            size = 4
            for w in shape[1:]:
                size *= w
            where[name] = o
            o += (size + 31) // 32 * 32
            return t

        where = {}
        X = take("x", [P, NT, D])
        hT_hi = take("hT_hi", [P, KD, TOK], F32R)
        hT_lo = take("hT_lo", [P, KD, TOK], F32R)
        raw = take("w_raw", [P, 2, KD, P])
        w_hi = take("w_hi", [P, 2, KD, P], F32R)
        w_lo = take("w_lo", [P, 2, KD, P], F32R)
        part = take("part", [P, NT, D])
        G = take("gate", [P, 2, D])
        gpost = take("g_post", [P, D])
        sg = take("silu_g", [P, TOK])
        ut = take("u_tmp", [P, TOK])
        ident = take("ident", [P, P])
        sel = take("sel", [MLH, MLH, P])
        mlmask = take("mlmask", [P, 2, P])
        namask = take("namask", [P, GRID_W])
        mcol = take("mod_cols", [P, 2, 2, 2, KD])
        gpre = take("g_pre", [P, 2, KD])
        ssq = take("ssq", [P, 2, NT])
        msq = take("msq", [P, 2, NT])
        rms = take("rms", [P, 2, NT])
        halfneg = take("minus_half", [P, 20])
        ccol = take("cond_cols", [P, 2, KD])
        csil = take("cond_silu", [P, 2, KD])
        cw = take("conv_w", [P, 3, KD])
        cb = take("conv_b", [P, KD])
        hnorm = take("hnorm", [P, MLH])
        gateb = take("gate_b", [MLH, 4])
        mprev = take("m_prev", [MLH, 2, NT])
        small = take("small", [P, 16])
        arena = o
        junk = at("junk", [P, D], where["silu_g"])

        act_hi = at("act_hi", [P, HF, TOK], arena, F32R)
        act_lo = at("act_lo", [P, HF, TOK], arena + HF * TOK * 4, F32R)
        conv_at = arena + 2 * KD * TOK * 4 + 6 * TOK * 4
        upad = at("u_pad", [P, TOK + 3], conv_at)
        yconv = at("y_conv", [P, TOK + 1], conv_at + (TOK + 16) * 4)
        assert conv_at + 2 * (TOK + 16) * 4 <= end
        h_mod = at("h_mod", [P, 2, KD, P], arena)
        ada = at("ada_raw", [P, 2, KD, MODW], arena)
        adab = at("ada_bias", [2, 2, MODW], arena + 2 * KD * MODW * 4)
        mrow = at("mod_row", [2, 2, MODW], arena + 2 * KD * MODW * 4 + 2 * MODW * 4)
        FT = at("featT", [P, 20, TOK], arena)
        a1 = arena + 20 * TOK * 4
        va = at("va_tok", [P, NT, NAH * NAD], a1)
        a2 = a1 + NT * NAH * NAD * 4
        kmt = at("km_tok", [P, NT, MLH, MLD], a2)
        a3 = a2 + NT * MLH * MLD * 4
        vmt = at("vm_tok", [P, NT, MLH, MLD + 1], a3)
        assert a3 + NT * MLH * (MLD + 1) * 4 <= end, (end - a3)
        kcT = at("kctxT", [P, NAH // 2, P], where["silu_g"])
        pt0 = where["part"]
        atok = at("attn_tok", [P, NT, NAH * NAD], pt0)
        hsum = at("h_sum", [P, NT, MLH, MLD], pt0)
        p1 = pt0 + NT * NAH * NAD * 4
        ftmp = at("feat_tmp", [P, 2, TOK], p1)
        ktok = at("kctx_tok", [P, NAH, NAD], p1 + 2 * TOK * 4)
        vctx = at("vctx_tok", [P, NAH, NAD], p1 + 2 * TOK * 4 + 2048)
        padsb = at("rpb_pad", [NAH * DR, PADW], p1 + 2 * TOK * 4 + 4096)
        hh = where["hT_hi"]
        T2 = at("bias", [P, 2, TJ, GRID_W], hh)
        Sb = at("probs", [P, 2, NT, P], hh + 2 * TJ * GRID_W * 4)
        PT = at("probsT", [P, 2, NT, P], hh + 2 * TJ * GRID_W * 4 + 2 * NT * P * 4)
        grow = at("gate_rows", [MLH, 4, TOK], arena)
        brow = at("b_rows", [MLH, 2, TOK], arena + 4 * TOK * 4)
        mrw = at("m_rows", [MLH, 2, TOK], arena + 6 * TOK * 4)
        erow = at("e_rows", [MLH, 2, TOK], a1)
        Mrow = at("M_rows", [MLH, 2, TOK], a1 + 2 * TOK * 4)
        graw = at("gates_raw", [NG, TOK], where["u_tmp"])
        half = KD // 2 * TOK * 4
        Wx = at("decay", [P, 2, MLH, P], hh + half)
        wi = at("w_inter", [P, 2, MLH, P], hh + half + 4096)
        htmp = at("h_tmp", [P, MLH, MLD], hh + half + 8192)
        hl = where["hT_lo"]
        STs = at("scoresT", [P, 2, MLH, P], hl + half)
        qs = at("q_scaled", [P, 2, MLH, P], hl + half + 4096)
        ecol = at("e_cols", [P, 2, 2, NT, MLH], hl + half + 8192)
        mpb = at("m_prev_b", [P, MLH, 2, NT], hl + half + 8192 + 320)
        hssq = at("h_ssq", [P, NT * MLH], hl + half + 8192 + 480)
        hms = at("h_ms", [P, NT * MLH], hl + half + 8192 + 576)
        hr = at("h_r", [P, NT * MLH], hl + half + 8192 + 672)
        den = at("den", [P, 2, MLH], hl + half + 8192 + 768)
        vw = at("v_weighted", [P, 2, MLH, MLD + 1], p1)
        Cs = at("C_state", [P, 2, MLH, MLD + 1], p1 + 2 * 2080)

        PS = ctx.enter_context(nc.psum_tensor("psum", [P, 8, 512], F32))
        pair = lambda b: PS[:, b:b + 2, :]
        IN = [pair(0), pair(2)]
        IN_V = [IN[p][:, :, 0:HT] for p in range(2)]
        flat = lambda ap: ap.rearrange("p a b -> p (a b)")
        TR = [flat(pair(6)).rearrange("p (k t) -> p k t", t=P), flat(pair(0)).rearrange("p (k t) -> p k t", t=P)]
        OUT = [[4, 5, 6, 7, 0], [1, 2, 3, 4, 5]]
        halves = lambda ap: ap.rearrange("p (a b) -> p a b", a=2)

        modd = nc.dram_tensor("modulation", (2, 2, NMOD), F32, kind="Internal").ap()
        biasd = nc.dram_tensor("bias_rep", (NAH * DR, GRID_W, PADW), F32, kind="Internal").ap()

        w_loaded = [sem("w_loaded0"), sem("w_loaded1")]
        w_hi_ok, w_lo_ok, pe_unit = sem("w_hi_ok"), sem("w_lo_ok"), sem("pe_unit")
        in_evac = [sem("in_evac0"), sem("in_evac1")]
        act_ready, out_ready, out_evac = sem("act_ready"), sem("out_ready"), sem("out_evac")
        ssq_post, r_post, x_new = sem("ssq_post"), sem("r_post"), sem("x_new")
        ssq_pre, r_pre, xh_ok, xT_ok = sem("ssq_pre"), sem("r_pre"), sem("xh_ok"), sem("xT_ok")
        hmod_ok, hhi_ok, hT_ready = sem("hmod_ok"), sem("hhi_ok"), sem("hT_ready")
        s_dve, s_pool = sem("s_dve"), sem("s_pool")
        s_const, s_x, s_c = sem("s_const"), sem("s_x"), sem("s_c")
        csil_ok, neg_ok = sem("csil_ok"), sem("neg_ok")
        ada_loaded = [sem("ada_loaded0"), sem("ada_loaded1")]
        mod_mm, mrow_ok = sem("mod_mm"), sem("mrow_ok")
        mod_stored = [sem("mod_stored0"), sem("mod_stored1")]
        cols_loaded, gate_loaded, mod_ready = sem("cols_loaded"), sem("gate_loaded"), sem("mod_ready")
        y_stored = sem("y_stored")
        u_split = sem("u_split")
        tr_done, tr_evac = sem("tr_done"), sem("tr_evac")
        pad_zero, pad_loaded, rep_stored = sem("pad_zero"), sem("pad_loaded"), sem("rep_stored")
        ctx_loaded, kc_done, kc_evac = sem("ctx_loaded"), sem("kc_done"), sem("kc_evac")
        bias_loaded = [sem("bias_loaded0"), sem("bias_loaded1")]
        bias_ok = sem("bias_ok")
        na_s, na_nm, na_p, na_t, na_pt, na_o, na_ok = (sem(n) for n in (
            "na_scores", "na_negmax", "na_probs", "na_transposed", "na_probsT", "na_out", "na_norm"))
        aT_done, aT_evac = sem("aT_done"), sem("aT_evac")
        kv_out, kv_done = sem("kv_out"), sem("kv_done")
        g_evac, g_moved, g_rows = sem("g_evac"), sem("g_moved"), sem("g_rows")
        st_loaded, m0_loaded = sem("st_loaded"), sem("m0_loaded")
        r_abs, r_exp, r_ln, r_m, r_em = sem("r_abs"), sem("r_exp"), sem("r_ln"), sem("r_m"), sem("r_em")
        r_mp, col_done, col_ok = sem("r_mp"), sem("col_done"), sem("col_ok")
        ml_rm, ml_x, ml_w, ml_wi, ml_qk, ml_st, ml_qs, ml_vw, ml_num, ml_c, ml_h, ml_cs = (sem(n) for n in (
            "ml_rm", "ml_x", "ml_w", "ml_wi", "ml_qk", "ml_st", "ml_qs", "ml_vw", "ml_num", "ml_c", "ml_h", "ml_cs"))
        ones_ok, st_out = sem("ones_ok"), sem("st_out")
        h_ssq_ok, h_r_ok, h_n_ok, hT2_done, hT2_evac = (sem(n) for n in (
            "h_ssq_ok", "h_r_ok", "h_n_ok", "hT2_done", "hT2_evac"))
        conv_zero = sem("conv_zero")

        NCH = NMOD // MODW
        plan = []
        ev, oe, ar = Evacs(), 0, 0
        for s, kind in enumerate(SUBS):
            b = UB[s]
            if kind == "ffn":
                ph = []
                for h in range(2):
                    iv = ev.phase(b, FFN_IN)
                    ph.append(dict(nin=b, iv=iv, iv_end=list(ev.n), nout=b + FFN_IN, oe=oe, ar=ar, k=HF, half=h))
                    b += FFN_IN + FFN_OUT
                    oe += 2 * NT
                    ar += HF
            elif kind == "ab":
                iv = ev.phase(b, AB_UNITS + 1)
                ph = [dict(nin=b, iv=iv, iv_end=list(ev.n), nout=b + AB_UNITS + 1, oe=oe, ar=ar, k=KD)]
                oe += 2 * NT
                ar += KD
            else:
                iv = ev.phase(b, SC_IN)
                ph = [dict(nin=b, iv=iv, iv_end=list(ev.n), nout=b + SC_IN, oe=oe, ar=ar, k=KD)]
                oe += 2 * NT
                ar += KD
            plan.append(ph)

        def inv(ph, n):
            first = ph["nin"] + ((n - ph["nin"]) % 2)
            return ph["iv"][n % 2] + (n - first) // 2 + 1

        OR = lambda ph, d, t: (ph["oe"] // NT + d) * (NT - 1) + t + 1

        NA_ITEMS = [(h, t) for h in range(NAH) for t in range(NT)]
        ML_STEPS = [(0, 0), (1, 3), (0, 1), (1, 2), (0, 2), (1, 1), (0, 3), (1, 0), (0, CT), (1, CT)]

        cond = lambda t: 1 if t == CT else 0
        xs = x_sample.rearrange("b (t p) d -> p (b t) d", p=P)
        xp = x_prompt.rearrange("b p d -> p b d")
        ys = y_sample.rearrange("b (t p) d -> p (b t) d", p=P)
        yp = y_prompt.rearrange("b p d -> p b d")

        block = ctx.enter_context(nc.Block())

        @block.sync
        def _(sp):
            dma = lambda out, in_, **kw: sp.dma_start(out, in_, **kw)
            slow = dict(allow_slow_non_contiguous=True)
            dma(ccol[:, 0, :], c.rearrange("b (p k) -> p (b k)", k=KD)).then_inc(s_c, 16)
            dma(ccol[:, 1, :], c_ctx.rearrange("(p k) -> p k", k=KD)).then_inc(s_c, 16)

            for l in range(2):
                def load_chunks(i):
                    for r in range(2):
                        need(sp, mod_mm, i * 2 + (l * NCH - 3 + r))
                        need(sp, mrow_ok, i * 2 + (l * NCH - 3 + r))
                        col = i * (2 * MODW) + (r - 2) * MODW
                        dma(ada[:, r], ada_w[l].rearrange("(p k) n -> p k n", k=KD)[:, :, bass.ds(col, MODW)]).then_inc(ada_loaded[r], 16)
                        dma(adab[:, r, :], bass.AP(ada_b.tensor, ada_b[l].offset, [[0, 2], [1, NMOD]])[:, bass.ds(col, MODW)]).then_inc(ada_loaded[r], 16)

                load_chunks(1)
                with sp.Fori(2, NCH // 2 + 1) as i:
                    load_chunks(i)
                if l == 0:
                    dma(X[:, 0:CT, :], xs).then_inc(s_x, 16)
                    dma(X[:, CT:NT, :], xp).then_inc(s_x, 16)
                    dma(ident[:], k_ident).then_inc(s_const, 16)
                    dma(sel[:], k_sel).then_inc(s_const, 16)
                    dma(mlmask[:], k_mlmask).then_inc(s_const, 16)
                    dma(namask[:], k_namask).then_inc(s_const, 16)
                    dma(cw[:], sc_conv_w[0].rearrange("w (k p) -> p w k", p=P), **slow).then_inc(s_const, 16)
                    dma(cb[:], sc_conv_b[0].rearrange("(k p) -> p k", p=P), **slow).then_inc(s_const, 16)
                    dma(hnorm[:], ml_hnorm[0].rearrange("(k p) -> p k", p=P), **slow).then_inc(s_const, 16)
                    dma(gateb[:], ml_gate_b[0].rearrange("a h -> h a"), **slow).then_inc(s_const, 16)
            sp.wait_ge(mod_stored[0], 16 * NCH)
            sp.wait_ge(mod_stored[1], 16 * NCH)

            def load_cols(s):
                l, j = s // 3, s % 3
                for kind in range(2):
                    src = bass.AP(modd.tensor, modd[l, 0, (3 * j + kind) * D:].offset, [[KD, P], [NMOD, 2], [1, KD]])
                    dma(mcol[:, s % 2, kind], src).then_inc(cols_loaded, 16)
                dma(gpre[:, s % 2, :], norm_g[l, j, 0].rearrange("(p k) -> p k", k=KD)).then_inc(cols_loaded, 16)

            def load_gate(s):
                l, j = s // 3, s % 3
                if s:
                    sp.wait_ge(x_new, NT * s)
                src = bass.AP(modd.tensor, modd[l, 0, (3 * j + 2) * D:].offset, [[0, P], [NMOD, 2], [1, D]])
                dma(G[:], src).then_inc(gate_loaded, 16)
                dma(gpost[:], bass.AP(norm_g.tensor, norm_g[l, j, 1].offset, [[0, P], [1, D]])).then_inc(gate_loaded, 16)

            load_cols(0)

            def load_in(w, nb, off, count, colof, stride):
                per = len(colof)

                def body(i):
                    for r, col in enumerate(colof):
                        n = nb + off + r
                        need(sp, w_lo_ok, i * per + (n - 1 - per))
                        dma(raw[:, n % 2], w.rearrange("(p k) n -> p k n", k=KD)[:, :, bass.ds(i * stride + (col - stride), P)]).then_inc(w_loaded[n % 2], 16)

                body(1)
                with sp.Fori(2, count + 1) as i:
                    body(i)

            def load_out(w, row0, ph):
                for d in range(2):
                    for k in range(ph["k"]):
                        n = ph["nout"] + d * ph["k"] + k
                        sp.wait_ge(w_lo_ok, n - 1)
                        dma(raw[:, n % 2, 0:4, :].rearrange("p a b -> p (a b)"),
                            w[row0 + k * P:row0 + (k + 1) * P, d * 512:(d + 1) * 512]).then_inc(w_loaded[n % 2], 16)

            for s, kind in enumerate(SUBS):
                l, f = s // 3, s % 3 // 2
                for ph in plan[s]:
                    nb = ph["nin"]
                    if kind == "ffn":
                        c0 = ph["half"] * HF * P
                        load_in(ffn_w13[l, f], nb, 0, HF, [FF + c0, c0], P)
                        if ph["half"] == 1:
                            load_gate(s)
                            if s + 1 < len(SUBS):
                                load_cols(s + 1)
                        load_out(ffn_w2[l, f], c0, ph)
                    elif kind == "sc":
                        cols = [D, 2 * D, 0, D + P, 2 * D + P, P]
                        load_in(sc_w_in[0], nb, 0, KD // 2, cols, 2 * P)
                        load_gate(s)
                        load_cols(s + 1)
                        load_out(sc_w_out[0], 0, ph)
                    else:
                        load_in(ab_w_in[0], nb, 0, AB_UNITS // 2, [0, P], 2 * P)
                        n = nb + AB_UNITS
                        sp.wait_ge(w_lo_ok, n - 1)
                        dma(raw[:, n % 2, :, 0:NG], ab_w_in[0].rearrange("(p k) n -> p k n", k=KD)[:, :, AB_IN - NG:]).then_inc(w_loaded[n % 2], 16)
                        sp.wait_ge(hT_ready, NT * (s + 1))
                        sp.wait_ge(pad_zero, 1)
                        dma(padsb[:, GRID_W - WIN_W:GRID_W - WIN_W + DC], na_rpb[0].rearrange("h r c -> (h r) c")).then_inc(pad_loaded, 16)
                        dma(ktok[:], cache_k[0, 0].rearrange("h p d -> p h d")).then_inc(ctx_loaded, 16)
                        dma(vctx[:], cache_v[0, 0].rearrange("h p d -> p h d")).then_inc(ctx_loaded, 16)
                        sp.wait_ge(pad_loaded, 16)
                        rep = padsb[:, :]
                        dma(biasd[:], bass.AP(rep.tensor, rep.offset, [rep.ap[0], [0, GRID_W], [1, PADW]])).then_inc(rep_stored, 16)
                        n = ph["nout"]
                        sp.wait_ge(w_lo_ok, n - 1)
                        dma(raw[:, n % 2, 0:4, :].rearrange("p a b -> p (a b)"), ab_w_out[0][0:P, 0:512]).then_inc(w_loaded[n % 2], 16)
                        sp.wait_ge(kv_out, 1)
                        dma(new_k[0, 0].rearrange("h p d -> p h d"), Sb[:, 0, 0:4, :].rearrange("p a b -> p (a b)").rearrange("p (h d) -> p h d", d=NAD)).then_inc(kv_done, 16)
                        dma(new_v[0, 0].rearrange("h p d -> p h d"), va[:, CT, :].rearrange("p (h d) -> p h d", d=NAD)).then_inc(kv_done, 16)
                        sp.wait_ge(rep_stored, 16)
                        sp.wait_ge(pe_unit, nb + AB_UNITS + 1)
                        for h in range(NAH):
                            if h >= 2:
                                sp.wait_ge(na_nm, NT * (h - 1))
                            for up in range(2):
                                row = h * DR + 1 - up
                                src = bass.AP(biasd.tensor, row * GRID_W * PADW + GRID_W - 1, [[PADW - 1, GRID_W], [GRID_W * PADW, TJ], [1, GRID_W]])
                                dma(T2[up * GRID_W:(up + 1) * GRID_W, h % 2], src).then_inc(bias_loaded[h % 2], 16)
                        sp.wait_ge(aT_evac, 2 * KD // 2)
                        sp.wait_ge(kv_done, 32)
                        for kd in range(4):
                            dma(grow[:, kd, :], graw[kd * MLH:(kd + 1) * MLH, :]).then_inc(g_moved, 16)
                        dma(mprev[:, 0, 0:1], state_m[0, 0, 0].rearrange("(h a) -> h a", a=1), **slow).then_inc(m0_loaded, 16)
                        dma(mprev[:, 1, CT - 1:CT], state_m[0, 0, 1].rearrange("(h a) -> h a", a=1), **slow).then_inc(m0_loaded, 16)
                        for dr in range(2):
                            dma(Cs[:, dr, :, 0:MLD], state_C[0, 0, dr].rearrange("h p e -> p h e")).then_inc(st_loaded, 16)
                            dma(Cs[:, dr, :, MLD:MLD + 1], state_n[0, 0, dr].rearrange("h (p a) -> p h a", a=1), **slow).then_inc(st_loaded, 16)
                        sp.wait_ge(r_m, 1)
                        dma(new_m[0, 0, 0].rearrange("(h a) -> h a", a=1), mrw[:, 0, TOK - 1:TOK], **slow).then_inc(st_out, 16)
                        dma(new_m[0, 0, 1].rearrange("(h a) -> h a", a=1), mrw[:, 1, LAT:LAT + 1], **slow).then_inc(st_out, 16)
                        for dr in range(2):
                            sp.wait_ge(ml_cs, 7 + dr)
                            dma(new_C[0, 0, dr].rearrange("h p e -> p h e"), Cs[:, dr, :, 0:MLD]).then_inc(st_out, 16)
                            dma(new_n[0, 0, dr].rearrange("h (p a) -> p h a", a=1), Cs[:, dr, :, MLD:MLD + 1], **slow).then_inc(st_out, 16)
                        sp.wait_ge(st_out, 16 * 6)
                        load_gate(s)
                        load_cols(s + 1)
                        for n2 in range(1, AB_OUT):
                            d, k = n2 // KD, n2 % KD
                            n = ph["nout"] + n2
                            sp.wait_ge(w_lo_ok, n - 1)
                            dma(raw[:, n % 2, 0:4, :].rearrange("p a b -> p (a b)"), ab_w_out[0][k * P:(k + 1) * P, d * 512:(d + 1) * 512]).then_inc(w_loaded[n % 2], 16)
            for t in range(NT):
                sp.wait_ge(x_new, NT * len(SUBS) - NT + t + 1 + 0)
                dst = ys[:, t, :] if t < CT else yp[:, 0, :]
                dma(dst, X[:, t, :]).then_inc(y_stored, 16)
            sp.wait_ge(y_stored, 16 * NT)

        @block.tensor
        def _(pe):
            mm = nc.tensor.matmul

            pe.wait_ge(csil_ok, 1)
            for l in range(2):
                def chunk_pair(i):
                    for r in range(2):
                        pe.wait_ge(ada_loaded[r], (i + 1 + l * (NCH // 2)) * 32)
                        need(pe, mrow_ok, i * 2 + (l * NCH + r - 1))
                        for k in range(KD):
                            last = mm(PS[0:2, r, :], csil[:, :, k], ada[:, r, k, :], start=(k == 0), stop=(k == KD - 1))
                        last.then_inc(mod_mm, 1)

                chunk_pair(0)
                with pe.Fori(1, NCH // 2) as i:
                    chunk_pair(i)

            def three(out, a_hi, a_lo, b_hi, b_lo, first, final):
                mm(out, a_hi, b_hi, start=first, stop=False)
                mm(out, a_hi, b_lo, start=False, stop=False)
                return mm(out, a_lo, b_hi, start=False, stop=final)

            def turn_x(s):
                if s == 0:
                    pe.wait_ge(s_const, 16 * 8)
                    pe.wait_ge(mrow_ok, 2 * NCH)
                else:
                    pe.wait_ge(out_evac, plan[s][0]["oe"])
                for t in range(NT):
                    pe.wait_ge(xh_ok, NT * s + t + 1)
                    if t >= 2:
                        pe.wait_ge(hT_ready, NT * s + t - 1)
                    for k in range(KD):
                        last = nc.tensor.transpose(TR[t % 2][:, k, :], part[:, t, k::KD], ident[:])
                    last.then_inc(xT_ok, 1)

            def in_unit(ph, r, i, per, width=P):
                n = ph["nin"] + r
                p = n % 2
                pe.wait_ge(w_lo_ok, n + 1 + i * per)
                need(pe, in_evac[p], inv(ph, n) - 1 + i * (per // 2))
                for k in range(KD):
                    hi, lo = w_hi[:, p, k, 0:width], w_lo[:, p, k, 0:width]
                    for a, b in ((hi, hT_hi), (hi, hT_lo), (lo, hT_hi)):
                        for h in range(2):
                            last = mm(IN[p][0:width, h, 0:HT], a, b[:, k, h * HT:(h + 1) * HT],
                                      start=(k == 0 and a is hi and b is hT_hi), stop=(k == KD - 1 and a is lo))
                last.then_inc(pe_unit, 1)

            def out_phase(ph, a_hi, a_lo):
                for d in range(2):
                    for k in range(ph["k"]):
                        n = ph["nout"] + d * ph["k"] + k
                        pe.wait_ge(w_lo_ok, n + 1)
                        if d == 0:
                            pe.wait_ge(act_ready, ph["ar"] + k + 1)
                            if k == 0:
                                pe.wait_ge(out_evac, ph["oe"])
                        for t in range(NT):
                            if k == 0 and d == 0 and t == NT - 1:
                                pe.wait_ge(in_evac[0], ph["iv_end"][0])
                            if k == 0 and d == 1:
                                if t == 0:
                                    pe.wait_ge(in_evac[0], ph["iv_end"][0])
                                    pe.wait_ge(in_evac[1], ph["iv_end"][1])
                                if t >= 3:
                                    pe.wait_ge(out_evac, ph["oe"] + t - 2)
                            tok = slice(t * P, (t + 1) * P)
                            b_hi = w_hi[:, n % 2, 0:4, :].rearrange("p a b -> p (a b)")
                            b_lo = w_lo[:, n % 2, 0:4, :].rearrange("p a b -> p (a b)")
                            last = three(PS[:, OUT[d][t], :], a_hi[:, k, tok], a_lo[:, k, tok], b_hi, b_lo, k == 0, k == ph["k"] - 1)
                            if k == ph["k"] - 1 and t < NT - 1:
                                last.then_inc(out_ready, 1)
                        last.then_inc(pe_unit, 1)

            def mixing(ph):
                s_base = ph["nin"]
                tr = 0

                def group(r0, turned):
                    nonlocal tr
                    def body(i):
                        in_unit(ph, r0, i, 2)
                        in_unit(ph, r0 + 1, i, 2)
                        if turned:
                            for r in range(2):
                                n = s_base + r0 + r
                                p = n % 2
                                pe.wait_ge(in_evac[p], inv(ph, n) + i)
                                need(pe, tr_evac, i * 2 + (tr + r - 1))
                                for t in range(NT):
                                    last = nc.tensor.transpose(PS[:, 4 + 2 * r + t // 4, (t % 4) * P:(t % 4 + 1) * P],
                                                               ftmp[:, p, t * P:(t + 1) * P], ident[:])
                                last.then_inc(tr_done, 1)

                    body(0)
                    with pe.Fori(1, 2) as i:
                        body(i)
                    if turned:
                        tr += 4

                group(0, False)
                group(4, False)
                group(8, True)
                group(12, False)
                group(16, True)
                group(20, True)
                group(24, False)
                in_unit(ph, AB_UNITS, 0, 2, NG)
                pe.wait_ge(ctx_loaded, 32)
                pe.wait_ge(tr_evac, tr)
                for a in range(4):
                    last = nc.tensor.transpose(PS[:, 4, a * P:(a + 1) * P], ktok[:, 2 * a:2 * a + 2, :].rearrange("p a b -> p (a b)"), ident[:])
                last.then_inc(kc_done, 1)
                for a in range(4):
                    last = nc.tensor.transpose(PS[:, 5, a * P:(a + 1) * P], FT[:, 4 + a, LAT:TOK], ident[:])
                last.then_inc(kc_done, 1)
                pe.wait_ge(kc_evac, 2)
                pe.wait_ge(in_evac[0], ph["iv_end"][0])
                pe.wait_ge(in_evac[1], ph["iv_end"][1])

                def scores(i):
                    h, t = NA_ITEMS[i]
                    pp = slice((h % 2) * NAD, (h % 2 + 1) * NAD)
                    if i >= 2:
                        pe.wait_ge(na_p, i - 1)
                    q = FT[pp, h // 2, t * P:(t + 1) * P]
                    b = 2 * (i % 2)
                    if t < CT:
                        mm(PS[:, b, :], q, FT[pp, 4 + h // 2, 0:LAT], start=True, stop=True)
                        last = mm(PS[:, b + 1, 0:P], q, kcT[pp, h // 2, :], start=True, stop=True)
                    else:
                        last = mm(PS[:, b + 1, 0:P], q, FT[pp, 4 + h // 2, LAT:TOK], start=True, stop=True)
                    last.then_inc(na_s, 1)

                def turn(i):
                    h, t = NA_ITEMS[i]
                    pe.wait_ge(na_p, i + 1)
                    if i:
                        pe.wait_ge(na_pt, i)
                    for a in (range(NT) if t < CT else [CT]):
                        last = nc.tensor.transpose(PS[:, 4 + a // 4, (a % 4) * P:(a % 4 + 1) * P], Sb[:, i % 2, a, :], ident[:])
                    last.then_inc(na_t, 1)

                def weigh(i):
                    h, t = NA_ITEMS[i]
                    pe.wait_ge(na_pt, i + 1)
                    if i >= 2:
                        pe.wait_ge(na_ok, i - 1)
                    tiles = range(NT) if t < CT else [CT]
                    for a in tiles:
                        v = va[:, a, h * NAD:(h + 1) * NAD] if t == CT or a < CT else vctx[:, h, :]
                        last = mm(PS[:, 6 + i % 2, 0:NAD], PT[:, i % 2, a, :], v, start=(a == tiles[0]), stop=(a == CT))
                    last.then_inc(na_o, 1)

                NI = len(NA_ITEMS)
                for i in range(NI + 2):
                    if i < NI:
                        scores(i)
                    if 1 <= i <= NI:
                        turn(i - 1)
                    if i >= 2:
                        weigh(i - 2)
                pe.wait_ge(na_ok, NI)
                for k in range(4):
                    if k >= 2:
                        pe.wait_ge(aT_evac, 2 * (k - 1))
                    for t in range(NT):
                        last = nc.tensor.transpose(PS[:, 2 * (k % 2) + t // 4, (t % 4) * P:(t % 4 + 1) * P], atok[:, t, k * P:(k + 1) * P], ident[:])
                    last.then_inc(aT_done, 1)

                pe.wait_ge(r_em, 1)
                pe.wait_ge(r_mp, 1)
                for qn, rows in enumerate((erow, brow)):
                    for dr in range(2):
                        for cc in range(NT):
                            col = ((qn * 2 + dr) * NT + cc) * MLH
                            nc.tensor.transpose(PS[:, 4, col:col + MLH], rows[:, dr, cc * P:(cc + 1) * P], ident[0:MLH, 0:MLH])
                for h in range(MLH):
                    last = mm(PS[:, 5, h * 2 * NT:(h + 1) * 2 * NT], sel[:, h, :], mprev[:].rearrange("p a b -> p (a b)"), start=True, stop=True)
                last.then_inc(col_done, 1)

                def front(q):
                    dr, cc = ML_STEPS[q]
                    if q < 2:
                        pe.wait_ge(aT_evac, 8)
                    else:
                        pe.wait_ge(ml_x, q - 1)
                        pe.wait_ge(ml_wi, q - 1)
                    for h in range(MLH):
                        last = mm(PS[:, q % 2, h * P:(h + 1) * P], sel[:, h, :], Mrow[:, dr, cc * P:(cc + 1) * P], start=True, stop=True)
                    last.then_inc(ml_rm, 1)
                    if q >= 2:
                        pe.wait_ge(ml_st, q - 1)
                    for h in range(MLH):
                        last = mm(PS[:, 2 + q % 2, h * P:(h + 1) * P], FT[:, 12 + h, cc * P:(cc + 1) * P], FT[:, 8 + h, cc * P:(cc + 1) * P], start=True, stop=True)
                    last.then_inc(ml_qk, 1)

                def back(q):
                    dr, cc = ML_STEPS[q]
                    inter = cc < CT
                    pe.wait_ge(ml_st, q + 1)
                    pe.wait_ge(ml_qs, min(q + 1, 8))
                    if q:
                        pe.wait_ge(ml_h, q)
                    else:
                        pe.wait_ge(col_ok, 1)
                        pe.wait_ge(st_loaded, 64)
                        pe.wait_ge(ones_ok, 1)
                    if q >= 2 and inter:
                        pe.wait_ge(ml_cs, q - 1)
                    for h in range(MLH):
                        o_ = PS[:, 4 + h // 2, (h % 2) * 256:(h % 2) * 256 + MLD + 1]
                        last = mm(o_, STs[:, q % 2, h, :], vmt[:, cc, h, :], start=True, stop=not inter)
                        if inter:
                            last = mm(o_, qs[:, q % 2, h, :], Cs[:, dr, h, :], start=False, stop=True)
                    last.then_inc(ml_num, 1)
                    if q in NEEDS_STATE:
                        j = NEEDS_STATE.index(q)
                        pe.wait_ge(ml_vw, j + 1)
                        if j:
                            pe.wait_ge(ml_cs, j)
                        for h in range(MLH):
                            last = mm(PS[:, 6 + h // 2, (h % 2) * 256:(h % 2) * 256 + MLD + 1], kmt[:, cc, h, :], vw[:, j % 2, h, :], start=True, stop=True)
                        last.then_inc(ml_c, 1)

                for q in range(len(ML_STEPS) + 1):
                    if q < len(ML_STEPS):
                        front(q)
                    if q:
                        back(q - 1)
                pe.wait_ge(h_n_ok, 1)
                for h in range(MLH):
                    if h >= 2:
                        pe.wait_ge(hT2_evac, h - 1)
                    for t in range(NT):
                        last = nc.tensor.transpose(PS[:, 2 * (h % 2) + t // 4, (t % 4) * P:(t % 4 + 1) * P], hsum[:, t, h, :], ident[:])
                    last.then_inc(hT2_done, 1)

            for s, kind in enumerate(SUBS):
                turn_x(s)
                pe.wait_ge(hT_ready, NT * (s + 1))
                for ph in plan[s]:
                    pe.wait_ge(out_evac, ph["oe"])
                    if kind == "ffn":
                        in_unit(ph, 0, 0, 2)
                        in_unit(ph, 1, 0, 2)
                        with pe.Fori(1, HF) as i:
                            in_unit(ph, 0, i, 2)
                            in_unit(ph, 1, i, 2)
                        out_phase(ph, act_hi, act_lo)
                    elif kind == "sc":
                        with pe.Fori(0, KD // 2) as i:
                            for r in range(6):
                                in_unit(ph, r, i, 6)
                        out_phase(ph, act_hi, act_lo)
                    else:
                        mixing(ph)
                        out_phase(ph, hT_hi, hT_lo)

        @block.scalar
        def _(act):
            A = nc.scalar.activation
            act.wait_ge(s_c, 32)
            A(csil[:], ccol[:], ACT.Silu).then_inc(csil_ok, 1)
            for l in range(2):
                with act.Fori(0, NCH // 2) as i:
                    for r in range(2):
                        act.wait_ge(mrow_ok, l * NCH + i * 2 + r + 1)
                        act.dma_start(modd[l, :, bass.ds(i * (2 * MODW) + r * MODW, MODW)], mrow[:, r, :]).then_inc(mod_stored[r], 16)

            def split(n, i=0, per=0, shape=None):
                act.wait_ge(w_loaded[n % 2], (n // 2 + 1 + i * (per // 2)) * 16)
                need(act, pe_unit, n - 1 + i * per)
                src, dst = raw[:, n % 2], w_hi[:, n % 2]
                if shape == "out":
                    src, dst = src[:, 0:4, :], dst[:, 0:4, :]
                elif shape == "gates":
                    src, dst = src[:, :, 0:NG], dst[:, :, 0:NG]
                A(dst, src, ACT.Copy).then_inc(w_hi_ok, 1)

            def pre(s):
                def square(t):
                    if s == 0:
                        act.wait_ge(s_x, 32)
                    else:
                        act.wait_ge(x_new, NT * (s - 1) + t + 1)
                    A(part[:, t, :], X[:, t, :], ACT.Square, accum_out=ssq[:, 0, t:t + 1]).then_inc(ssq_pre, 1)

                def normalise(t):
                    act.wait_ge(r_pre, NT * s + t + 1)
                    A(part[:, t, :], X[:, t, :], ACT.Copy, scale=rms[:, 0, t:t + 1]).then_inc(xh_ok, 1)

                def take_hi(t):
                    act.wait_ge(hmod_ok, NT * s + t + 1)
                    A(hT_hi[:, :, t * P:(t + 1) * P], h_mod[:, t % 2], ACT.Copy).then_inc(hhi_ok, 1)

                for q in range(NT + 3):
                    if q < NT:
                        if s:
                            t = q
                            ph = plan[s - 1][-1]
                            act.wait_ge(out_evac, ph["oe"] + NT + t + 1)
                            if t:
                                act.wait_ge(ssq_post, NT * (s - 1) + t)
                            A(junk[:], part[:, t, :], ACT.Square, accum_out=ssq[:, 1, t:t + 1]).then_inc(ssq_post, 1)
                    if 1 <= q <= NT:
                        square(q - 1)
                    if 2 <= q <= NT + 1:
                        normalise(q - 2)
                    if q >= 3:
                        take_hi(q - 3)

            def last_post(s):
                ph = plan[s][-1]
                for t in range(NT):
                    act.wait_ge(out_evac, ph["oe"] + NT + t + 1)
                    if t:
                        act.wait_ge(ssq_post, NT * s + t)
                    A(junk[:], part[:, t, :], ACT.Square, accum_out=ssq[:, 1, t:t + 1]).then_inc(ssq_post, 1)

            def out_splits(ph, nxt):
                total = 2 * ph["k"]
                for u in range(1, total):
                    split(ph["nout"] + u, shape="out")
                if nxt:
                    split(ph["nout"] + total)

            def ffn_in(ph):
                nb = ph["nin"]
                ffn_pair(ph, nb, 0, False)
                with act.Fori(1, HF - 1) as i:
                    ffn_pair(ph, nb, i, False)
                ffn_pair(ph, nb, HF - 1, True)

            def ffn_pair(ph, nb, i, last):
                split(nb + 1, i, 2)
                act.wait_ge(pe_unit, nb + 1 + i * 2)
                need(act, in_evac[(nb + 1) % 2], inv(ph, nb + 1) - 1 + i)
                A(halves(sg[:]), IN_V[nb % 2], ACT.Silu).then_inc(in_evac[nb % 2], 1)
                split(nb + 2, i, 2, shape="out" if last else None)

            def sc_in(ph):
                nb = ph["nin"]

                def body(i, last):
                    for r in range(6):
                        fin = last and r == 5
                        split(nb + r + 1, i, 6, shape="out" if fin else None)
                        if r % 3 == 0:
                            act.wait_ge(pe_unit, nb + r + 1 + i * 6)
                            if r == 0:
                                act.wait_ge(act_ready, ph["ar"] + i * 2)
                            else:
                                act.wait_ge(act_ready, ph["ar"] + 1 + i * 2)
                            A(halves(sg[:]), IN_V[(nb + r) % 2], ACT.Copy).then_inc(in_evac[(nb + r) % 2], 1)

                with act.Fori(0, KD // 2 - 1) as i:
                    body(i, False)
                body(KD // 2 - 1, True)

            def mixing(ph):
                nb = ph["nin"]
                tr = 0

                def group(r0, dst, scale=None, func=ACT.Copy, turned=False, last=False):
                    nonlocal tr

                    def body(i):
                        for r in range(2):
                            n = nb + r0 + r
                            p = n % 2
                            fin = last and r == 1
                            split(n + 1, i, 2)
                            act.wait_ge(pe_unit, n + 1 + i * 2)
                            kw = {} if scale is None else {"scale": scale}
                            if turned:
                                need(act, tr_done, i * 2 + (tr + r - 1))
                                a = A(halves(ftmp[:, p, :]), IN_V[p], func, **kw)
                            if dst is not None:
                                a = A(FT[:, bass.ds(i * 2 + dst + r, 1), :].rearrange("p a (b c) -> p (a b) c", b=2), IN_V[p], func, **kw)
                            a.then_inc(in_evac[p], 1)

                    body(0)
                    with act.Fori(1, 2) as i:
                        body(i)
                    if turned:
                        tr += 4

                group(0, 0, scale=NAD ** -0.5)
                group(4, 4)
                group(8, None, turned=True)
                group(12, 8)
                group(16, 12, scale=MLD ** -0.5, turned=True)
                group(20, None, turned=True)
                for r in range(4):
                    n = nb + 24 + r
                    split(n + 1, shape="gates" if r == 3 else None)
                    act.wait_ge(pe_unit, n + 1)
                    A(FT[:, 16 + r, :].rearrange("p (b c) -> p b c", b=2), IN_V[n % 2], ACT.Sigmoid).then_inc(in_evac[n % 2], 1)
                n = nb + AB_UNITS
                split(n + 1, shape="out")
                act.wait_ge(pe_unit, n + 1)
                A(halves(graw[:]), IN_V[n % 2][0:NG], ACT.Copy).then_inc(in_evac[n % 2], 1)
                act.wait_ge(kc_done, 1)
                A(kcT[:].rearrange("p a b -> p (a b)"), PS[:, 4, :], ACT.Copy).then_inc(kc_evac, 1)
                for i, (h, t) in enumerate(NA_ITEMS):
                    act.wait_ge(na_nm, i + 1)
                    if i >= 2:
                        act.wait_ge(na_t, i - 1)
                    nm = small[:, 4 * (i % 2) + 2:4 * (i % 2) + 3]
                    dd = small[:, 8 + 2 * (i % 4):8 + 2 * (i % 4) + 2]
                    if i >= 4:
                        act.wait_ge(na_ok, i - 3)
                    if t < CT:
                        p_loc = Sb[:, i % 2, 0:4, :].rearrange("p a b -> p (a b)")
                        A(p_loc, p_loc, ACT.Exp, bias=nm, accum_out=dd[:, 0:1])
                    A(Sb[:, i % 2, CT, :], PS[:, 2 * (i % 2) + 1, 0:P], ACT.Exp, bias=nm, accum_out=dd[:, 1:2]).then_inc(na_p, 1)
                act.wait_ge(g_rows, 1)
                fg = grow[:, 1::2, :]
                lg = Mrow[:, :, :]
                A(lg, fg, ACT.Abs).then_inc(r_abs, 1)
                act.wait_ge(r_abs, 1)
                A(lg, lg, ACT.Exp, scale=-1.0).then_inc(r_exp, 1)
                act.wait_ge(r_exp, 1)
                A(lg, lg, ACT.Ln, bias=1.0).then_inc(r_ln, 1)
                act.wait_ge(r_m, 1)
                A(brow[:], mrw[:], ACT.Exp, scale=-1.0).then_inc(r_em, 1)
                for q, (dr, cc) in enumerate(ML_STEPS):
                    act.wait_ge(ml_x, q + 1)
                    if q == 0:
                        act.wait_ge(col_ok, 1)
                    if q >= 2:
                        act.wait_ge(ml_h, q - 1)
                        act.wait_ge(ml_qs, min(q - 1, 8))
                        act.wait_ge(ml_vw, sum(1 for z in NEEDS_STATE if z < q - 1))
                        act.wait_ge(ml_cs, sum(1 for z in NEEDS_STATE if z < q - 1))
                    for h in range(MLH):
                        last = A(wi[:, q % 2, h, :], PS[:, q % 2, h * P:(h + 1) * P], ACT.Exp, scale=-1.0, bias=mpb[:, h, dr, cc:cc + 1])
                    last.then_inc(ml_wi, 1)
                    A(Wx[:, q % 2], Wx[:, q % 2], ACT.Exp, scale=-1.0).then_inc(ml_w, 1)

            split(0)
            for s, kind in enumerate(SUBS):
                pre(s)
                for ph in plan[s]:
                    if kind == "ffn":
                        ffn_in(ph)
                    elif kind == "sc":
                        sc_in(ph)
                    else:
                        mixing(ph)
                    out_splits(ph, not (s == len(SUBS) - 1 and ph is plan[s][-1]))
            last_post(len(SUBS) - 1)

        @block.gpsimd
        def _(pool):
            own = Steps(pool, s_pool)
            pool.memset(halfneg[:], -0.5).then_inc(neg_ok, 1)
            pool.wait_ge(neg_ok, 1)

            def rsqrt(dst, tmp, src, width, scale):
                own.link(pool.tensor_scalar(tmp, src, scale, EPS, ALU.mult, ALU.add))
                return pool.tensor_tensor(dst, tmp, halfneg[:, 0:width], ALU.pow)

            def post_r(s, t):
                pool.wait_ge(ssq_post, NT * s + t + 1)
                rsqrt(rms[:, 1, t:t + 1], msq[:, 1, t:t + 1], ssq[:, 1, t:t + 1], 1, 1.0 / D).then_inc(r_post, 1)

            def pre_r(s, t):
                pool.wait_ge(ssq_pre, NT * s + t + 1)
                rsqrt(rms[:, 0, t:t + 1], msq[:, 0, t:t + 1], ssq[:, 0, t:t + 1], 1, 1.0 / D).then_inc(r_pre, 1)

            for s, kind in enumerate(SUBS):
                for q in range(NT + 1):
                    if s and q < NT:
                        post_r(s - 1, q)
                    if q:
                        pre_r(s, q - 1)
                if kind == "sc":
                    pool.wait_ge(hT_ready, NT * (s + 1))
                    pool.memset(upad[:], 0.0).then_inc(conv_zero, 1)
                if kind == "ab":
                    pool.wait_ge(hT_ready, NT * (s + 1))
                    pool.memset(padsb[:], 0.0).then_inc(pad_zero, 1)
                    pool.memset(vmt[:, :, :, MLD:MLD + 1], 1.0).then_inc(ones_ok, 1)
                    pool.wait_ge(ones_ok, 1)
                    nv = 0
                    for q, (dr, cc) in enumerate(ML_STEPS):
                        edge = P - 1 if dr == 0 else 0
                        if cc < CT:
                            pool.wait_ge(ml_wi, q + 1)
                            if q >= 2:
                                pool.wait_ge(ml_num, q - 1)
                            pool.tensor_tensor(qs[:, q % 2], FT[:, 8:12, cc * P:(cc + 1) * P], wi[:, q % 2], ALU.mult).then_inc(ml_qs, 1)
                        if q in NEEDS_STATE:
                            pool.wait_ge(ml_w, q + 1)
                            if nv >= 2:
                                pool.wait_ge(ml_c, nv - 1)
                            wl = Wx[:, q % 2, :, edge:edge + 1].to_broadcast([P, MLH, MLD + 1])
                            pool.tensor_tensor(vw[:, nv % 2], vmt[:, cc], wl, ALU.mult).then_inc(ml_vw, 1)
                            nv += 1
                    pool.wait_ge(h_ssq_ok, 1)
                    rsqrt(hr[:], hms[:], hssq[:], NT * MLH, 1.0 / MLD).then_inc(h_r_ok, 1)
            for t in range(NT):
                post_r(len(SUBS) - 1, t)

        @block.vector
        def _(dve):
            own = Steps(dve, s_dve)
            V = nc.vector
            for l in range(2):
                def rows(i):
                    for r in range(2):
                        dve.wait_ge(mod_mm, l * NCH + i * 2 + r + 1)
                        need(dve, mod_stored[r], (i + l * (NCH // 2)) * 16)
                        V.tensor_tensor(mrow[:, r, :], PS[0:2, r, :], adab[:, r, :], ALU.add).then_inc(mrow_ok, 1)

                rows(0)
                with dve.Fori(1, NCH // 2) as i:
                    rows(i)

            def split(n, i=0, per=0, shape=None):
                dve.wait_ge(w_hi_ok, n + 1 + i * per)
                a, b, d_ = raw[:, n % 2], w_hi[:, n % 2], w_lo[:, n % 2]
                if shape == "out":
                    a, b, d_ = (z[:, 0:4, :] for z in (a, b, d_))
                elif shape == "gates":
                    a, b, d_ = (z[:, :, 0:NG] for z in (a, b, d_))
                V.tensor_tensor(d_, a, b.bitcast(F32), ALU.subtract).then_inc(w_lo_ok, 1)

            def scale_cols(s):
                dve.wait_ge(cols_loaded, 48 * (s + 1))
                m = mcol[:, s % 2, 1]
                g = gpre[:, s % 2, None, :].to_broadcast([P, 2, KD])
                own.link(V.scalar_tensor_tensor(m, m, 1.0, g, ALU.add, ALU.mult))

            def gate_tile(s):
                dve.wait_ge(gate_loaded, 32 * (s + 1))
                w = 1.0 if s % 3 == 1 else 0.5
                own.link(V.scalar_tensor_tensor(G[:], G[:], w, gpost[:, None, :].to_broadcast([P, 2, D]), ALU.mult, ALU.mult))

            def add_out(s, t):
                dve.wait_ge(r_post, NT * s + t + 1)
                own.link(V.scalar_tensor_tensor(part[:, t, :], part[:, t, :], rms[:, 1, t:t + 1], G[:, cond(t), :], ALU.mult, ALU.mult))
                V.tensor_tensor(X[:, t, :], X[:, t, :], part[:, t, :], ALU.add).then_inc(x_new, 1)

            def modulate(s, t):
                dve.wait_ge(xT_ok, NT * s + t + 1)
                b = t % 2
                sc_ = mcol[:, s % 2, 1, cond(t), :, None].to_broadcast([P, KD, P])
                sh_ = mcol[:, s % 2, 0, cond(t), :, None].to_broadcast([P, KD, P])
                own.link(V.tensor_tensor(h_mod[:, b], TR[b], sc_, ALU.mult))
                V.tensor_tensor(h_mod[:, b], h_mod[:, b], sh_, ALU.add).then_inc(hmod_ok, 1)

            def take_lo(s, t):
                tok = slice(t * P, (t + 1) * P)
                dve.wait_ge(hhi_ok, NT * s + t + 1)
                V.tensor_tensor(hT_lo[:, :, tok], h_mod[:, t % 2], hT_hi[:, :, tok].bitcast(F32), ALU.subtract).then_inc(hT_ready, 1)

            def pre(s):
                for q in range(NT + 3):
                    if s and q < NT:
                        add_out(s - 1, q)
                    if q >= 3:
                        take_lo(s, q - 3)
                    if 2 <= q <= NT + 1:
                        modulate(s, q - 2)

            def evac_out(ph, add):
                def evac(d):
                    for t in range(NT):
                        if t < NT - 1:
                            dve.wait_ge(out_ready, OR(ph, d, t))
                        else:
                            dve.wait_ge(pe_unit, ph["nout"] + (d + 1) * ph["k"])
                        dst = part[:, t, d * 512:(d + 1) * 512]
                        src = PS[:, OUT[d][t], :]
                        if add:
                            V.tensor_tensor(dst, src, dst, ALU.add).then_inc(out_evac, 1)
                        else:
                            V.tensor_copy(dst, src).then_inc(out_evac, 1)
                return evac

            def out_phase(s, ph, nxt):
                K = ph["k"]
                evac = evac_out(ph, ph.get("half") == 1)
                for u in range(1, 2 * K):
                    split(ph["nout"] + u, shape="out")
                    if u == K:
                        evac(0)
                    if u == K + 2 and ph is plan[s][-1]:
                        gate_tile(s)
                        if s + 1 < len(SUBS):
                            scale_cols(s + 1)
                if nxt:
                    split(ph["nout"] + 2 * K)
                evac(1)

            def split_act(k, hi, lo, src, i=0):
                own.link(V.tensor_copy(hi, src))
                V.tensor_tensor(lo, src, hi.bitcast(F32), ALU.subtract).then_inc(act_ready, 1)

            def ffn_pair(ph, i, last):
                nb = ph["nin"]
                split(nb + 1, i, 2)
                split(nb + 2, i, 2, shape="out" if last else None)
                dve.wait_ge(pe_unit, nb + 2 + i * 2)
                dve.wait_ge(in_evac[nb % 2], inv(ph, nb) + i)
                need(dve, act_ready, ph["ar"] + i)
                p = (nb + 1) % 2
                V.tensor_tensor(halves(ut[:]), IN_V[p], halves(sg[:]), ALU.mult).then_inc(in_evac[p], 1)
                dve.wait_ge(in_evac[p], inv(ph, nb + 1) + i)
                if isinstance(i, int):
                    hi, lo = act_hi[:, i, :], act_lo[:, i, :]
                    u = ut[:]
                else:
                    hi, lo, u = act_hi[:, bass.ds(i, 1), :], act_lo[:, bass.ds(i, 1), :], ut[:, None, :]
                split_act(i, hi, lo, u)

            def ffn_in(ph):
                ffn_pair(ph, 0, False)
                with own.loop(1, HF - 1, 1) as i:
                    ffn_pair(ph, i, False)
                ffn_pair(ph, HF - 1, True)

            def sc_in(ph):
                nb = ph["nin"]
                dve.wait_ge(conv_zero, 1)
                pieces = [(0, 0, 0, HT), (1, 0, HT, LAT), (1, LAT - HT, LAT, TOK)]

                def body(i, last):
                    for jj in range(2):
                        n = nb + 3 * jj
                        split(n + 1, i, 6)
                        split(n + 2, i, 6)
                        dve.wait_ge(pe_unit, n + 2 + i * 6)
                        dve.wait_ge(in_evac[n % 2], inv(ph, n) + i * 3)
                        for z, (h, f0, t0, t1) in enumerate(pieces):
                            off = 1 if t0 < LAT else 2
                            ins = V.tensor_tensor(upad[:, t0 + off:t1 + off], IN_V[(n + 1) % 2][:, h, f0:f0 + t1 - t0], sg[:, t0:t1], ALU.mult)
                        ins.then_inc(in_evac[(n + 1) % 2], 1)
                        dve.wait_ge(in_evac[(n + 1) % 2], inv(ph, n + 1) + i * 3)
                        col = lambda ap: ap[:, bass.ds(i * 2 + jj, 1)]
                        own.link(V.tensor_scalar(yconv[:], upad[:, 1:TOK + 2], col(cw[:, 1, :]), col(cb[:, :]), ALU.mult, ALU.add))
                        own.link(V.scalar_tensor_tensor(yconv[:], upad[:, 0:TOK + 1], col(cw[:, 0, :]), yconv[:], ALU.mult, ALU.add))
                        own.link(V.scalar_tensor_tensor(yconv[:], upad[:, 2:TOK + 3], col(cw[:, 2, :]), yconv[:], ALU.mult, ALU.add))
                        split(n + 3, i, 6, shape="out" if last and jj == 1 else None)
                        dve.wait_ge(pe_unit, n + 3 + i * 6)
                        for z, (h, f0, t0, t1) in enumerate(pieces):
                            off = 0 if t0 < LAT else 1
                            ins = V.tensor_tensor(ut[:, t0:t1], IN_V[n % 2][:, h, f0:f0 + t1 - t0], yconv[:, t0 + off:t1 + off], ALU.mult)
                        ins.then_inc(in_evac[n % 2], 1)
                        dve.wait_ge(in_evac[n % 2], inv(ph, n + 2) + i * 3)
                        hi, lo = (z[:, bass.ds(i * 2 + jj, 1), :] for z in (act_hi, act_lo))
                        split_act(None, hi, lo, ut[:, None, :])
                        dve.wait_ge(act_ready, ph["ar"] + jj + 1 + i * 2)

                with own.loop(0, KD // 2 - 1, 8) as i:
                    body(i, False)
                body(KD // 2 - 1, True)

            def mixing(ph):
                nb = ph["nin"]
                tr = 0
                for g, dst in enumerate((None, None, "va", None, "km", "vm", None)):
                    rolled = 2 if g < 6 else 1
                    with dve.Fori(0, rolled) as i:
                        for r in range(2):
                            split(nb + 4 * g + r + 1, i, 2)
                        if dst:
                            for r in range(2):
                                dve.wait_ge(tr_done, tr + r + 1 + i * 2)
                                src = flat(pair(4 + 2 * r))[:, 0:TOK].rearrange("p (t e) -> p t e", e=P)
                                if dst == "va":
                                    o_ = va[:, :, bass.ds(i * (2 * P) + r * P, P)]
                                else:
                                    z = kmt if dst == "km" else vmt
                                    o_ = z[:, :, bass.ds(i * 2 + r, 1), 0:MLD].rearrange("p t a e -> p t (a e)")
                                V.tensor_copy(o_, src).then_inc(tr_evac, 1)
                    if dst:
                        tr += 4
                split(nb + 27)
                split(nb + 28, shape="gates")
                split(nb + 29, shape="out")
                dve.wait_ge(kc_done, 2)
                own.link(V.tensor_copy(Sb[:, 0, 0:4, :].rearrange("p a b -> p (a b)"), PS[:, 5, :]))
                dve.sem_inc(kc_evac, 1)
                dve.sem_inc(kv_out, 1)

                def masked(h):
                    dve.wait_ge(bias_loaded[h % 2], 32 * (h // 2 + 1))
                    own.link(V.tensor_tensor(T2[:, h % 2], T2[:, h % 2], namask[:, None, :].to_broadcast([P, TJ, GRID_W]), ALU.add))

                def maxima(i):
                    h, t = NA_ITEMS[i]
                    if t == 0:
                        masked(h)
                    dve.wait_ge(na_s, i + 1)
                    if i == 0:
                        dve.wait_ge(kv_done, 32)
                        dve.wait_ge(kv_out, 1)
                    if i >= 2:
                        dve.wait_ge(na_t, i - 1)
                        dve.wait_ge(na_p, i - 1)
                    m = small[:, 4 * (i % 2):4 * (i % 2) + 4]
                    ctx_s = PS[:, 2 * (i % 2) + 1, 0:P]
                    if t < CT:
                        off = (ROWS - 2 - 2 * t)
                        bias = T2[:, h % 2, off:off + ROWS, :].rearrange("p a b -> p (a b)")
                        V.tensor_tensor_reduce(Sb[:, i % 2, 0:4, :].rearrange("p a b -> p (a b)"), PS[:, 2 * (i % 2), :], bias, 1.0, -BIG * 10, ALU.add, ALU.max, m[:, 0:1])
                        own.link(V.tensor_reduce(m[:, 1:2], ctx_s, AX.X, ALU.max))
                        V.tensor_scalar(m[:, 2:3], m[:, 0:1], m[:, 1:2], -1.0, ALU.max, ALU.mult).then_inc(na_nm, 1)
                    else:
                        own.link(V.tensor_reduce(m[:, 1:2], ctx_s, AX.X, ALU.max))
                        V.tensor_scalar(m[:, 2:3], m[:, 1:2], -1.0, None, ALU.mult).then_inc(na_nm, 1)

                def evac_T(i):
                    h, t = NA_ITEMS[i]
                    dve.wait_ge(na_t, i + 1)
                    if i >= 2:
                        dve.wait_ge(na_o, i - 1)
                    if t < CT:
                        V.tensor_copy(PT[:, i % 2].rearrange("p a b -> p (a b)"), flat(pair(4))[:, 0:TOK]).then_inc(na_pt, 1)
                    else:
                        V.tensor_copy(PT[:, i % 2, CT, :], PS[:, 5, 0:P]).then_inc(na_pt, 1)

                def divide(i):
                    h, t = NA_ITEMS[i]
                    dd = small[:, 8 + 2 * (i % 4):8 + 2 * (i % 4) + 2]
                    dve.wait_ge(na_o, i + 1)
                    if t < CT:
                        own.link(V.tensor_tensor(dd[:, 0:1], dd[:, 0:1], dd[:, 1:2], ALU.add))
                        own.link(V.reciprocal(dd[:, 0:1], dd[:, 0:1]))
                    else:
                        own.link(V.reciprocal(dd[:, 0:1], dd[:, 1:2]))
                    V.tensor_scalar(atok[:, t, h * NAD:(h + 1) * NAD], PS[:, 6 + i % 2, 0:NAD], dd[:, 0:1], None, ALU.mult).then_inc(na_ok, 1)

                NI = len(NA_ITEMS)
                for i in range(NI + 2):
                    if i < NI:
                        maxima(i)
                    if 1 <= i <= NI:
                        evac_T(i - 1)
                    if i >= 2:
                        divide(i - 2)
                aT = lambda k: flat(pair(2 * (k % 2)))[:, 0:TOK]
                for k in range(4):
                    dve.wait_ge(aT_done, k + 1)
                    V.tensor_copy(hT_hi[:, k, :], aT(k)).then_inc(aT_evac, 1)
                    dve.wait_ge(aT_evac, 2 * k + 1)
                    V.tensor_tensor(hT_lo[:, k, :], aT(k), hT_hi[:, k, :].bitcast(F32), ALU.subtract).then_inc(aT_evac, 1)

                dve.wait_ge(g_moved, 64)
                own.link(V.tensor_tensor(grow[:], grow[:], gateb[:, :, None].to_broadcast([MLH, 4, TOK]), ALU.add))
                V.memset(mprev[:, :, CT:NT], 0.0).then_inc(g_rows, 1)
                fg, ig = grow[:, 1::2, :], grow[:, 0::2, :]
                dve.wait_ge(r_ln, 1)
                own.link(V.scalar_tensor_tensor(fg, fg, 0.0, Mrow[:], ALU.min, ALU.subtract))
                rev = lambda ap: ap[:, ::-1]
                for dr in range(2):
                    way = rev if dr else (lambda ap: ap)
                    for cc in range(NT):
                        f = way(grow[:, 2 * dr + 1, cc * P:(cc + 1) * P])
                        last = V.tensor_tensor_scan(way(brow[:, dr, cc * P:(cc + 1) * P]), f, f, 0.0, ALU.add, ALU.min)
                own.link(last)
                dve.wait_ge(m0_loaded, 32)
                dve.wait_ge(g_rows, 1)
                for dr in range(2):
                    way = rev if dr else (lambda ap: ap)
                    for lo_, hi_, m0 in ((0, LAT, mprev[:, dr, 0:1] if dr == 0 else mprev[:, dr, CT - 1:CT]), (LAT, TOK, 0.0)):
                        last = V.tensor_tensor_scan(way(mrw[:, dr, lo_:hi_]), way(grow[:, 2 * dr + 1, lo_:hi_]), way(grow[:, 2 * dr, lo_:hi_]), m0, ALU.add, ALU.max)
                own.link(last)
                own.link(V.tensor_tensor(erow[:], ig, brow[:], ALU.subtract))
                own.link(V.tensor_tensor(Mrow[:], mrw[:], brow[:], ALU.subtract))
                V.tensor_copy(mprev[:, 0, 1:CT], mrw[:, 0, P - 1:LAT - P:P])
                own.link(V.tensor_copy(mprev[:, 1, 0:CT - 1], mrw[:, 1, P:LAT:P]))
                dve.sem_inc(r_m, 1)
                dve.sem_inc(r_mp, 1)
                dve.wait_ge(col_done, 1)
                own.link(V.tensor_copy(ecol[:].rearrange("p a b c d -> p (a b c d)"), PS[:, 4, 0:4 * NT * MLH]))
                V.tensor_copy(mpb[:].rearrange("p a b c -> p (a b c)"), PS[:, 5, 0:2 * NT * MLH]).then_inc(col_ok, 1)

                seen = set()

                def decay(q):
                    dr, cc = ML_STEPS[q]
                    dve.wait_ge(ml_rm, q + 1)
                    if q >= 2:
                        dve.wait_ge(ml_st, q - 1)
                        dve.wait_ge(ml_vw, sum(1 for z in NEEDS_STATE if z < q - 1))
                    e = ecol[:, 0, dr, cc, :, None].to_broadcast([P, MLH, P])
                    rm = PS[:, q % 2, :].rearrange("p (h t) -> p h t", h=MLH)
                    own.link(V.tensor_tensor(Wx[:, q % 2], rm, e, ALU.subtract))
                    V.tensor_tensor(Wx[:, q % 2], Wx[:, q % 2], mlmask[:, dr, None, :].to_broadcast([P, MLH, P]), ALU.add).then_inc(ml_x, 1)

                def finish(q):
                    dr, cc = ML_STEPS[q]
                    edge = P - 1 if dr == 0 else 0
                    dve.wait_ge(ml_w, q + 1)
                    dve.wait_ge(ml_qk, q + 1)
                    if q >= 2:
                        dve.wait_ge(ml_num, q - 1)
                    V.tensor_tensor(STs[:, q % 2], PS[:, 2 + q % 2, :].rearrange("p (h t) -> p h t", h=MLH), Wx[:, q % 2], ALU.mult).then_inc(ml_st, 1)
                    dve.wait_ge(ml_num, q + 1)
                    num = pair(4).rearrange("p a (b c) -> p (a b) c", b=2)
                    dn = den[:, q % 2, :]
                    own.link(V.tensor_tensor(dn, num[:, :, MLD], ecol[:, 1, dr, cc, :], ALU.max))
                    own.link(V.scalar_tensor_tensor(dn, num[:, :, MLD], -1.0, dn, ALU.mult, ALU.max))
                    own.link(V.reciprocal(dn, dn))
                    r_ = den[:, q % 2, :, None].to_broadcast([P, MLH, MLD])
                    if cc in seen:
                        own.link(V.tensor_tensor(htmp[:], num[:, :, 0:MLD], r_, ALU.mult))
                        V.tensor_tensor(hsum[:, cc], hsum[:, cc], htmp[:], ALU.add).then_inc(ml_h, 1)
                    else:
                        seen.add(cc)
                        V.tensor_tensor(hsum[:, cc], num[:, :, 0:MLD], r_, ALU.mult).then_inc(ml_h, 1)
                    if q in NEEDS_STATE:
                        j = NEEDS_STATE.index(q)
                        dve.wait_ge(ml_c, j + 1)
                        dve.wait_ge(ml_wi, q + 1)
                        cu = pair(6).rearrange("p a (b c) -> p (a b) c", b=2)[:, :, 0:MLD + 1]
                        if cc < CT:
                            for h in range(MLH):
                                last = V.scalar_tensor_tensor(Cs[:, dr, h, :], Cs[:, dr, h, :], wi[:, q % 2, h, edge:edge + 1], cu[:, h, :], ALU.mult, ALU.add)
                        else:
                            last = V.tensor_copy(Cs[:, dr], cu)
                        last.then_inc(ml_cs, 1)

                decay(0)
                for q in range(len(ML_STEPS)):
                    if q + 1 < len(ML_STEPS):
                        decay(q + 1)
                    finish(q)
                dve.wait_ge(ml_h, len(ML_STEPS))
                for t in range(NT):
                    for h in range(MLH):
                        last = V.tensor_tensor_reduce(htmp[:, h, :], hsum[:, t, h, :], hsum[:, t, h, :], 1.0, 0.0, ALU.mult, ALU.add, hssq[:, t * MLH + h:t * MLH + h + 1])
                        own.link(last)
                dve.sem_inc(h_ssq_ok, 1)
                dve.wait_ge(h_r_ok, 1)
                hv = hsum[:].rearrange("p t h e -> p (t h) e")
                V.tensor_tensor(hv, hv, hr[:, :, None].to_broadcast([P, NT * MLH, MLD]), ALU.mult).then_inc(h_n_ok, 1)
                dve.wait_ge(in_evac[0], ph["iv_end"][0])
                for h in range(MLH):
                    dve.wait_ge(hT2_done, h + 1)
                    V.scalar_tensor_tensor(ut[:], aT(h), hnorm[:, h:h + 1], FT[:, 16 + h, :], ALU.mult, ALU.mult).then_inc(hT2_evac, 1)
                    dve.wait_ge(hT2_evac, h + 1)
                    own.link(V.tensor_copy(hT_hi[:, 4 + h, :], ut[:]))
                    own.link(V.tensor_tensor(hT_lo[:, 4 + h, :], ut[:], hT_hi[:, 4 + h, :].bitcast(F32), ALU.subtract))
                dve.sem_inc(act_ready, KD)

            split(0)
            scale_cols(0)
            for s, kind in enumerate(SUBS):
                pre(s)
                for ph in plan[s]:
                    if kind == "ffn":
                        ffn_in(ph)
                    elif kind == "sc":
                        sc_in(ph)
                    else:
                        mixing(ph)
                    out_phase(s, ph, not (s == len(SUBS) - 1 and ph is plan[s][-1]))
            for t in range(NT):
                add_out(len(SUBS) - 1, t)


NEEDS_STATE = [0, 1, 2, 3, 4, 5, 8, 9]

_INS = ['x_prompt', 'x_sample', 'cache_k', 'cache_v', 'state_C', 'state_n', 'state_m', 'c', 'c_ctx', 'ada_w',
        'ada_b', 'norm_g', 'ffn_w13', 'ffn_w2', 'ab_w_in', 'ab_w_out', 'na_rpb', 'ml_gate_b', 'ml_hnorm',
        'sc_w_in', 'sc_conv_w', 'sc_conv_b', 'sc_w_out']
_OUTS = [(1, 128, 1024), (1, 512, 1024), (1, 1, 8, 128, 64), (1, 1, 8, 128, 64), (1, 1, 2, 4, 128, 128),
         (1, 1, 2, 4, 128), (1, 1, 2, 4)]


def constants():
    import numpy as np
    ident = np.eye(P, dtype=np.float32)
    sel = np.zeros((MLH, MLH, P), np.float32)
    for h in range(MLH):
        sel[h, h, :] = 1.0
    s, t = np.arange(P)[:, None], np.arange(P)[None, :]
    mlmask = np.stack([np.where(s <= t, 0.0, BIG), np.where(s >= t, 0.0, BIG)], axis=1).astype(np.float32)
    q, k = np.arange(P)[:, None] % GRID_W, np.arange(GRID_W)[None, :]
    c0 = np.clip(q - WIN_W // 2, 0, GRID_W - WIN_W)
    namask = np.where((k >= c0) & (k < c0 + WIN_W), 0.0, -BIG).astype(np.float32)
    return {"k_ident": ident, "k_sel": sel, "k_mlmask": mlmask, "k_namask": namask}


def kernel(**inputs):
    import numpy as _np
    import concourse.bacc as _bacc
    from concourse import mybir as _mybir
    from concourse.bass_utils import run_bass_kernel_spmd as _run

    nc = _bacc.Bacc("TRN2", target_bir_lowering=False, num_devices=1)
    arrays, args = {}, []
    data = {name: _np.ascontiguousarray(inputs[name]) for name in _INS}
    data.update(constants())
    for name, a in data.items():
        arrays[f"in_{name}_dram"] = a
        args.append(nc.dram_tensor(f"in_{name}_dram", a.shape, _mybir.dt.from_np(a.dtype), kind="ExternalInput").ap())
    for i, shape in enumerate(_OUTS):
        args.append(nc.dram_tensor(f"out_{i}_dram", shape, _mybir.dt.float32, kind="ExternalOutput").ap())
    build(nc, *args)
    r = _run(nc, [arrays], core_ids=[0])
    return tuple(r.results[0][f"out_{i}_dram"] for i in range(len(_OUTS)))
```

```python
from contextlib import ExitStack, contextmanager

import concourse.bass as bass
from concourse import mybir

F32 = mybir.dt.float32
F32R = mybir.dt.float32r
ALU = mybir.AluOpType
ACT = mybir.ActivationFunctionType
AX = mybir.AxisListType
P = 128

D = 1024
LAT, CTX = 512, 128
TOK = LAT + CTX
NT = TOK // P
CT = LAT // P
KD = D // P
HT = TOK // 2
FF = 2816
HF = FF // P // 2
NMOD = 9 * D
MODW = 512
PRO = 2 * D // MODW
JW = 256
EPS = 1e-6
NAH, NAD = 8, 64
MLH, MLD = 4, 128
GRID_W, ROWS = 64, LAT // 64
WIN_H, WIN_W = 8, 16
DR, DC = 2 * WIN_H - 1, 2 * WIN_W - 1
PADW = 2 * GRID_W - 1
TJ = ROWS + 2 * (CT - 1)
BIG = 1e30
AB_IN = 3 * NAH * NAD + 4 * MLH * MLD + 4 * MLH
NG = 4 * MLH
SUBS = ["ffn", "ab", "ffn", "ffn", "sc", "ffn"]

FFN_IN, FFN_OUT = 2 * HF, 2 * HF
AB_UNITS = (AB_IN - NG) // P
AB_OUT = 2 * KD
SC_IN, SC_OUT = 3 * KD, 2 * KD
COUNT = {"ffn": 2 * (FFN_IN + FFN_OUT), "ab": AB_UNITS + 1 + AB_OUT, "sc": SC_IN + SC_OUT}
JOBS = {0: (0, 2 * D, (HF, HF), (3, 3)), 2: (1, 0, (HF, HF), (1, 1)), 3: (1, 6 * D, (HF, 0), (1, 0))}
for _s, _cols in ((0, NMOD - 2 * D), (2, 6 * D), (3, 3 * D)):
    assert (sum(JOBS[_s][2]) + sum(JOBS[_s][3])) * JW == _cols
UB = [sum(COUNT[k] for k in SUBS[:s]) for s in range(len(SUBS) + 1)]


class Steps:

    def __init__(self, eng, sem):
        self.eng, self.sem, self.n, self.off = eng, sem, 0, 0

    def link(self, ins):
        self.n += 1
        ins.then_inc(self.sem, 1)
        self.eng.wait_ge(self.sem, self.n + self.off)

    def mark(self, ins):
        self.n += 1
        ins.then_inc(self.sem, 1)

    def wait_back(self, k):
        self.eng.wait_ge(self.sem, self.n - k + self.off)

    @contextmanager
    def loop(self, start, end, per):
        n0 = self.n
        with self.eng.Fori(start, end) as i:
            self.off = (i - start) * per
            yield i
            assert self.n - n0 == per, (self.n - n0, per)
        self.n, self.off = n0 + per * (end - start), 0


def first(i):
    return isinstance(i, int) and i == 0


def need(eng, sem, n):
    if not isinstance(n, int) or n > 0:
        eng.wait_ge(sem, n)


class Evacs:

    def __init__(self):
        self.n = [0, 0]

    def phase(self, base, units):
        start = list(self.n)
        for u in range(base, base + units):
            self.n[u % 2] += 1
        return start


def build(nc, x_prompt, x_sample, cache_k, cache_v, state_C, state_n, state_m, c, c_ctx, ada_w,
          ada_b, norm_g, ffn_w13, ffn_w2, ab_w_in, ab_w_out, na_rpb, ml_gate_b, ml_hnorm, sc_w_in,
          sc_conv_w, sc_conv_b, sc_w_out, k_ident, k_sel, k_mlmask, k_namask,
          y_prompt, y_sample, new_k, new_v, new_C, new_n, new_m):
    ctx = ExitStack()
    with ctx:
        sb = lambda name, shape, dt=F32: ctx.enter_context(nc.sbuf_tensor(name, shape, dt))
        sem = lambda name: ctx.enter_context(nc.semaphore(name))
        at = lambda name, shape, off, dt=F32: nc.alloc_sbuf_tensor_at(name, shape, dt, offset=off)

        base = nc.sbuf_base
        base = (base + 31) // 32 * 32
        end = nc.sbuf_usable_end
        o = base

        def take(name, shape, dt=F32):
            nonlocal o
            t = at(name, shape, o, dt)
            size = 4
            for w in shape[1:]:
                size *= w
            where[name] = o
            o += (size + 31) // 32 * 32
            return t

        where = {}
        X = take("x", [P, NT, D])
        hT_hi = take("hT_hi", [P, KD, TOK], F32R)
        hT_lo = take("hT_lo", [P, KD, TOK], F32R)
        raw = take("w_raw", [P, 2, KD, P])
        w_hi = take("w_hi", [P, 2, KD, P], F32R)
        w_lo = take("w_lo", [P, 2, KD, P], F32R)
        part = take("part", [P, NT, D])
        G = take("gate", [P, 2, D])
        gpost = take("g_post", [P, D])
        sg = take("silu_g", [P, TOK])
        ut = take("u_tmp", [P, TOK])
        ident = take("ident", [P, P])
        sel = take("sel", [MLH, MLH, P])
        mlmask = take("mlmask", [P, 2, P])
        namask = take("namask", [P, GRID_W])
        mcol = take("mod_cols", [P, 2, 2, 2, KD])
        gpre = take("g_pre", [P, 2, KD])
        ssq = take("mean_sq", [P, 3, NT])
        msq = take("mean_sq_eps", [P, 3, NT])
        rms = take("rms", [P, 2, NT])
        diag = take("diag", [P, 2, P])
        ones = take("ones", [P, 1])
        halfneg = take("minus_half", [P, 20])
        ccol = take("cond_cols", [P, 2, KD])
        csil = take("cond_silu", [P, 2, KD])
        cw = take("conv_w", [P, 3, KD])
        cb = take("conv_b", [P, KD])
        hnorm = take("hnorm", [P, MLH])
        gateb = take("gate_b", [MLH, 4])
        mprev = take("m_prev", [MLH, 2, NT])
        small = take("small", [P, 16])
        arena = o
        junk = at("junk", [P, D], where["silu_g"])

        act_hi = at("act_hi", [P, HF, TOK], arena, F32R)
        act_lo = at("act_lo", [P, HF, TOK], arena + HF * TOK * 4, F32R)
        conv_at = arena + 2 * KD * TOK * 4 + 6 * TOK * 4
        upad = at("u_pad", [P, TOK + 3], conv_at)
        yconv = at("y_conv", [P, TOK + 1], conv_at + (TOK + 16) * 4)
        assert conv_at + 2 * (TOK + 16) * 4 <= end
        h_mod = at("h_mod", [P, 2, KD, P], arena)
        ada0 = at("ada_first", [P, PRO, KD, MODW], arena)
        adab0 = at("ada_bias_first", [2, PRO * MODW], where["part"])
        mrow0 = at("mod_row_first", [2, PRO, MODW], where["part"] + PRO * MODW * 4)
        assert arena + PRO * KD * MODW * 4 <= end
        j0 = arena + 2 * HF * TOK * 4
        ada = at("ada_raw", [P, 2, KD // 2, JW], j0)
        acc = at("mod_acc", [P, 2, JW], j0 + KD * JW * 4)
        mrow = at("mod_row", [1, 2, JW], j0 + (KD + 2) * JW * 4)
        adab = at("ada_bias", [1, JW], j0 + (KD + 4) * JW * 4)
        assert j0 + (KD + 5) * JW * 4 <= end
        FT = at("featT", [P, 20, TOK], arena)
        a1 = arena + 20 * TOK * 4
        va = at("va_tok", [P, NT, NAH * NAD], a1)
        a2 = a1 + NT * NAH * NAD * 4
        kmt = at("km_tok", [P, NT, MLH, MLD], a2)
        a3 = a2 + NT * MLH * MLD * 4
        vmt = at("vm_tok", [P, NT, MLH, MLD + 1], a3)
        assert a3 + NT * MLH * (MLD + 1) * 4 <= end, (end - a3)
        kcT = at("kctxT", [P, NAH // 2, P], where["silu_g"])
        pt0 = where["part"]
        atok = at("attn_tok", [P, NT, NAH * NAD], pt0)
        hsum = at("h_sum", [P, NT, MLH, MLD], pt0)
        p1 = pt0 + NT * NAH * NAD * 4
        ftmp = at("feat_tmp", [P, 2, TOK], p1)
        ktok = at("kctx_tok", [P, NAH, NAD], p1 + 2 * TOK * 4)
        vctx = at("vctx_tok", [P, NAH, NAD], p1 + 2 * TOK * 4 + 2048)
        padsb = at("rpb_pad", [NAH * DR, PADW], p1 + 2 * TOK * 4 + 4096)
        hh = where["hT_hi"]
        T2 = at("bias", [P, 2, TJ, GRID_W], hh)
        Sb = at("probs", [P, 2, NT, P], hh + 2 * TJ * GRID_W * 4)
        PT = at("probsT", [P, 2, NT, P], hh + 2 * TJ * GRID_W * 4 + 2 * NT * P * 4)
        grow = at("gate_rows", [MLH, 4, TOK], where["hT_lo"] + KD // 2 * TOK * 4)
        brow = at("b_rows", [MLH, 2, TOK], where["hT_lo"])
        mrw = at("m_rows", [MLH, 2, TOK], where["hT_lo"] + 2 * TOK * 4)
        Mrow = at("M_rows", [MLH, 2, TOK], a1)
        emrow = at("em_rows", [MLH, 2, TOK], a1 + 2 * TOK * 4)
        graw = at("gates_raw", [NG, TOK], where["u_tmp"])
        half = KD // 2 * TOK * 4
        Wx = at("decay", [P, 2, MLH, P], hh + half)
        wi = at("w_inter", [P, 2, MLH, P], hh + half + 4096)
        htmp = at("h_tmp", [P, MLH, MLD], hh + half + 8192)
        hl = where["hT_lo"]
        STs = at("scoresT", [P, 2, MLH, P], hl + half)
        qs = at("q_scaled", [P, 2, MLH, P], hl + half + 4096)
        ecol = at("e_cols", [P, 2, 2, NT, MLH], hl + half + 8192)
        mpb = at("m_prev_b", [P, MLH, 2, NT], hl + half + 8192 + 320)
        hssq = at("h_ssq", [P, NT * MLH], hl + half + 8192 + 480)
        hms = at("h_ms", [P, NT * MLH], hl + half + 8192 + 576)
        hr = at("h_r", [P, NT * MLH], hl + half + 8192 + 672)
        den = at("den", [P, 2, MLH], hl + half + 8192 + 768)
        vw = at("v_weighted", [P, 2, MLH, MLD + 1], p1)
        Cs = at("C_state", [P, 2, MLH, MLD + 1], p1 + 2 * 2080)

        PS = ctx.enter_context(nc.psum_tensor("psum", [P, 8, 512], F32))
        pair = lambda b: PS[:, b:b + 2, :]
        IN = [pair(0), pair(2)]
        IN_V = [IN[p][:, :, 0:HT] for p in range(2)]
        flat = lambda ap: ap.rearrange("p a b -> p (a b)")
        TR = [flat(pair(6)).rearrange("p (k t) -> p k t", t=P), flat(pair(4)).rearrange("p (k t) -> p k t", t=P)]
        MODSUM = 7
        OUT = [[4, 5, 6, 7, 0], [1, 2, 3, 4, 5]]
        halves = lambda ap: ap.rearrange("p (a b) -> p a b", a=2)

        modd = nc.dram_tensor("modulation", (2, 2, NMOD), F32, kind="Internal").ap()
        biasd = nc.dram_tensor("bias_rep", (NAH * DR, GRID_W, PADW), F32, kind="Internal").ap()

        w_loaded = [sem("w_loaded0"), sem("w_loaded1")]
        w_hi_ok, w_lo_ok, pe_unit = sem("w_hi_ok"), sem("w_lo_ok"), sem("pe_unit")
        in_evac = [sem("in_evac0"), sem("in_evac1")]
        act_ready, out_ready, out_evac = sem("act_ready"), sem("out_ready"), sem("out_evac")
        ssq_post, r_post, x_new = sem("ssq_post"), sem("r_post"), sem("x_new")
        ssq_half, gated_half, gated = sem("ssq_half"), sem("gated_half"), sem("gated")
        ssq_pre, diag_ok, xT_ok = sem("ssq_pre"), sem("diag_ok"), sem("xT_ok")
        hmod_ok, hT_ready = sem("hmod_ok"), sem("hT_ready")
        s_dve, s_pool = sem("s_dve"), sem("s_pool")
        s_ident, s_const, s_slow, s_x, s_c = sem("s_ident"), sem("s_const"), sem("s_slow"), sem("s_x"), sem("s_c")
        csil_ok, neg_ok = sem("csil_ok"), sem("neg_ok")
        first_loaded = [[sem(f"first_loaded{i}{h}") for h in range(2)] for i in range(PRO)]
        firstb_loaded, first_mm, first_row = (sem(n) for n in (
            "firstb_loaded", "first_mm", "first_row"))
        ada_loaded = [sem("ada_loaded0"), sem("ada_loaded1")]
        ada_used = [sem("ada_used0"), sem("ada_used1")]
        bias_in, mod_sum, mrow_ok, mod_stored = (sem(n) for n in ("bias_in", "mod_sum", "mrow_ok", "mod_stored"))
        cols_loaded, cols_ready, gate_loaded, gate_ready = (sem(n) for n in (
            "cols_loaded", "cols_ready", "gate_loaded", "gate_ready"))
        y_stored = sem("y_stored")
        tr_done, tr_evac = sem("tr_done"), sem("tr_evac")
        pad_zero, pad_loaded, rep_stored = sem("pad_zero"), sem("pad_loaded"), sem("rep_stored")
        ctx_loaded, kc_done, kc_evac = sem("ctx_loaded"), sem("kc_done"), sem("kc_evac")
        bias_loaded = [sem("bias_loaded0"), sem("bias_loaded1")]
        bias_ok = sem("bias_ok")
        na_s, na_nm, na_p, na_t, na_pt, na_o, na_ok = (sem(n) for n in (
            "na_scores", "na_negmax", "na_probs", "na_transposed", "na_probsT", "na_out", "na_norm"))
        aT_done, aT_evac = sem("aT_done"), sem("aT_evac")
        kv_out, kv_done = sem("kv_out"), sem("kv_done")
        g_evac, g_moved, g_rows = sem("g_evac"), sem("g_moved"), sem("g_rows")
        st_loaded, m0_loaded = sem("st_loaded"), sem("m0_loaded")
        r_abs, r_exp, r_ln, r_m, r_em = sem("r_abs"), sem("r_exp"), sem("r_ln"), sem("r_m"), sem("r_em")
        r_mp, col_done, col_ok = sem("r_mp"), sem("col_done"), sem("col_ok")
        ml_rm, ml_x, ml_w, ml_wi, ml_qk, ml_st, ml_qs, ml_vw, ml_num, ml_c, ml_h, ml_cs = (sem(n) for n in (
            "ml_rm", "ml_x", "ml_w", "ml_wi", "ml_qk", "ml_st", "ml_qs", "ml_vw", "ml_num", "ml_c", "ml_h", "ml_cs"))
        ones_ok, st_out = sem("ones_ok"), sem("st_out")
        h_ssq_ok, h_r_ok, h_n_ok, hT2_done, hT2_evac = (sem(n) for n in (
            "h_ssq_ok", "h_r_ok", "h_n_ok", "hT2_done", "hT2_evac"))
        conv_zero = sem("conv_zero")

        plan = []
        ev, oe, ar, jb = Evacs(), 0, 0, 0
        for s, kind in enumerate(SUBS):
            b = UB[s]
            if kind == "ffn":
                ph = []
                for h in range(2):
                    iv = ev.phase(b, FFN_IN)
                    ph.append(dict(nin=b, iv=iv, iv_end=list(ev.n), nout=b + FFN_IN, oe=oe, ar=ar, k=HF, half=h,
                                   jobs=JOBS[s][2][h] if s in JOBS else 0, late=JOBS[s][3][h] if s in JOBS else 0, jb=jb,
                                   layer=JOBS[s][0] if s in JOBS else 0, col=jcol if h else (JOBS[s][1] if s in JOBS else 0)))
                    jb += ph[-1]["jobs"] + ph[-1]["late"]
                    jcol = ph[-1]["col"] + (ph[-1]["jobs"] + ph[-1]["late"]) * JW
                    b += FFN_IN + FFN_OUT
                    oe += 2 * NT
                    ar += HF
            elif kind == "ab":
                iv = ev.phase(b, AB_UNITS + 1)
                ph = [dict(nin=b, iv=iv, iv_end=list(ev.n), nout=b + AB_UNITS + 1, oe=oe, ar=ar, k=KD)]
                oe += 2 * NT
                ar += KD
            else:
                iv = ev.phase(b, SC_IN)
                ph = [dict(nin=b, iv=iv, iv_end=list(ev.n), nout=b + SC_IN, oe=oe, ar=ar, k=KD)]
                oe += 2 * NT
                ar += KD
            plan.append(ph)

        def inv(ph, n):
            first = ph["nin"] + ((n - ph["nin"]) % 2)
            return ph["iv"][n % 2] + (n - first) // 2 + 1

        OR = lambda ph, d, t: (ph["oe"] // NT + d) * (NT - 1) + t + 1

        NA_ITEMS = [(h, t) for h in range(NAH) for t in range(NT)]
        ML_STEPS = [(0, 0), (1, 3), (0, 1), (1, 2), (0, 2), (1, 1), (0, 3), (1, 0), (0, CT), (1, CT)]

        cond = lambda t: 1 if t == CT else 0
        xs = x_sample.rearrange("b (t p) d -> p (b t) d", p=P)
        xp = x_prompt.rearrange("b p d -> p b d")
        ys = y_sample.rearrange("b (t p) d -> p (b t) d", p=P)
        yp = y_prompt.rearrange("b p d -> p b d")

        block = ctx.enter_context(nc.Block())

        @block.sync
        def _(sp):
            dma = lambda out, in_, **kw: sp.dma_start(out, in_, **kw)
            slow = dict(allow_slow_non_contiguous=True)
            dma(ccol[:, 0, :], c.rearrange("b (p k) -> p (b k)", k=KD)).then_inc(s_c, 16)
            dma(ccol[:, 1, :], c_ctx.rearrange("(p k) -> p k", k=KD)).then_inc(s_c, 16)

            dma(adab0[:], bass.AP(ada_b.tensor, ada_b[0].offset, [[0, 2], [1, PRO * MODW]])).then_inc(firstb_loaded, 16)
            for i in range(PRO):
                for h in range(2):
                    ks = slice(h * KD // 2, (h + 1) * KD // 2)
                    dma(ada0[:, i, ks, :], ada_w[0].rearrange("(p k) n -> p k n", k=KD)[:, ks, i * MODW:(i + 1) * MODW]).then_inc(first_loaded[i][h], 16)
            dma(X[:, 0:CT, :], xs).then_inc(s_x, 16)
            dma(X[:, CT:NT, :], xp).then_inc(s_x, 16)
            dma(ident[:], k_ident).then_inc(s_ident, 16)
            dma(raw[:, 0], ffn_w13[0, 0].rearrange("(p k) n -> p k n", k=KD)[:, :, FF:FF + P]).then_inc(w_loaded[0], 16)
            dma(raw[:, 1], ffn_w13[0, 0].rearrange("(p k) n -> p k n", k=KD)[:, :, 0:P]).then_inc(w_loaded[1], 16)
            dma(gpre[:, 0, :], norm_g[0, 0, 0].rearrange("(p k) -> p k", k=KD)).then_inc(cols_loaded, 16)
            dma(sel[:], k_sel).then_inc(s_const, 16)
            dma(mlmask[:], k_mlmask).then_inc(s_const, 16)
            dma(namask[:], k_namask).then_inc(s_const, 16)

            def load_slow():
                dma(cw[:], sc_conv_w[0].rearrange("w (k p) -> p w k", p=P), **slow).then_inc(s_slow, 16)
                dma(cb[:], sc_conv_b[0].rearrange("(k p) -> p k", p=P), **slow).then_inc(s_slow, 16)
                dma(hnorm[:], ml_hnorm[0].rearrange("(k p) -> p k", p=P), **slow).then_inc(s_slow, 16)
                dma(gateb[:], ml_gate_b[0].rearrange("a h -> h a"), **slow).then_inc(s_slow, 16)

            def load_job(ph, q, i=0):
                j = ph["jb"] + q
                col = i * JW + (ph["col"] + q * JW)
                w = ada_w[ph["layer"]].rearrange("(p h k) n -> p h k n", h=2, k=KD // 2)
                if j == 0:
                    sp.wait_ge(first_mm, PRO)
                for h in range(2):
                    need(sp, ada_used[h], i + j)
                    dma(ada[:, h], w[:, h, :, bass.ds(col, JW)]).then_inc(ada_loaded[h], 16)

            def load_bias(ph, q, i=0, stored=True):
                j = ph["jb"] + q
                col = i * JW + (ph["col"] + q * JW)
                need(sp, mrow_ok, i + j)
                dma(adab[:], ada_b[ph["layer"]].rearrange("(a n) -> a n", a=1)[:, bass.ds(col, JW)]).then_inc(bias_in, 16)
                if stored:
                    store_row(ph, q - 1, i)

            def store_row(ph, q, i=0):
                sp.wait_ge(mrow_ok, i + (ph["jb"] + q + 1))
                col = i * JW + (ph["col"] + q * JW)
                dma(modd[ph["layer"], None, :, bass.ds(col, JW)], mrow[:]).then_inc(mod_stored, 16)

            def load_cols(s):
                l, j = s // 3, s % 3
                for kind in range(2):
                    src = bass.AP(modd.tensor, modd[l, 0, (3 * j + kind) * D:].offset, [[KD, P], [NMOD, 2], [1, KD]])
                    dma(mcol[:, s % 2, kind], src).then_inc(cols_loaded, 16)
                dma(gpre[:, s % 2, :], norm_g[l, j, 0].rearrange("(p k) -> p k", k=KD)).then_inc(cols_loaded, 16)

            def load_gate(s):
                l, j = s // 3, s % 3
                if s:
                    sp.wait_ge(x_new, NT * s)
                src = bass.AP(modd.tensor, modd[l, 0, (3 * j + 2) * D:].offset, [[0, P], [NMOD, 2], [1, D]])
                dma(G[:], src).then_inc(gate_loaded, 16)
                dma(gpost[:], bass.AP(norm_g.tensor, norm_g[l, j, 1].offset, [[0, P], [1, D]])).then_inc(gate_loaded, 16)

            def load_in(w, nb, off, count, colof, stride, ph=None):
                per = len(colof)


                def body(i):
                    for r, col in enumerate(colof):
                        n = nb + off + r
                        need(sp, w_lo_ok, i * per + (n - 1 - per))
                        dma(raw[:, n % 2], w.rearrange("(p k) n -> p k n", k=KD)[:, :, bass.ds(i * stride + (col - stride), P)]).then_inc(w_loaded[n % 2], 16)

                jobs = ph is not None and ph["jobs"]
                if nb:
                    body(1)
                if jobs:
                    load_job(ph, 0)
                    body(2)
                    load_bias(ph, 0, stored=False)
                    load_job(ph, 1)
                with sp.Fori(3 if jobs else 2, count + 1) as i:
                    body(i)
                    if jobs:
                        load_bias(ph, -2, i)
                        load_job(ph, -1, i)

            def load_out(w, row0, ph):
                for d in range(2):
                    for k in range(ph["k"]):
                        n = ph["nout"] + d * ph["k"] + k
                        u = d * ph["k"] + k
                        jobs, late = ph.get("jobs", 0), ph.get("late", 0)
                        if u == 0 and jobs:
                            load_bias(ph, jobs - 1)
                        if u == 3 and jobs:
                            store_row(ph, jobs - 1)
                        z, r = divmod(u - ph["k"] - 1, 3)
                        if r == 0 and 0 <= z < late:
                            load_job(ph, jobs + z)
                        if r == 2 and 0 <= z < late:
                            load_bias(ph, jobs + z, stored=z > 0)
                        sp.wait_ge(w_lo_ok, n - 1)
                        dma(raw[:, n % 2, 0:4, :].rearrange("p a b -> p (a b)"),
                            w[row0 + k * P:row0 + (k + 1) * P, d * 512:(d + 1) * 512]).then_inc(w_loaded[n % 2], 16)

            for s, kind in enumerate(SUBS):
                l, f = s // 3, s % 3 // 2
                for ph in plan[s]:
                    nb = ph["nin"]
                    if kind == "ffn":
                        c0 = ph["half"] * HF * P
                        load_in(ffn_w13[l, f], nb, 0, HF, [FF + c0, c0], P, ph)
                        if ph["half"] == 1:
                            sp.wait_ge(mod_stored, 16 * (ph["jb"] + max(ph["jobs"] - 2, 0)))
                            load_gate(s)
                            if s + 1 < len(SUBS):
                                load_cols(s + 1)
                        elif s == 0:
                            load_slow()
                        load_out(ffn_w2[l, f], c0, ph)
                        if ph["late"]:
                            store_row(ph, ph["jobs"] + ph["late"] - 1)
                    elif kind == "sc":
                        cols = [D, 2 * D, 0, D + P, 2 * D + P, P]
                        load_in(sc_w_in[0], nb, 0, KD // 2, cols, 2 * P)
                        load_gate(s)
                        load_cols(s + 1)
                        load_out(sc_w_out[0], 0, ph)
                    else:
                        load_in(ab_w_in[0], nb, 0, AB_UNITS // 2, [0, P], 2 * P)
                        n = nb + AB_UNITS
                        sp.wait_ge(w_lo_ok, n - 1)
                        dma(raw[:, n % 2, :, 0:NG], ab_w_in[0].rearrange("(p k) n -> p k n", k=KD)[:, :, AB_IN - NG:]).then_inc(w_loaded[n % 2], 16)
                        sp.wait_ge(hT_ready, NT * (s + 1))
                        sp.wait_ge(pad_zero, 1)
                        dma(padsb[:, GRID_W - WIN_W:GRID_W - WIN_W + DC], na_rpb[0].rearrange("h r c -> (h r) c")).then_inc(pad_loaded, 16)
                        dma(ktok[:], cache_k[0, 0].rearrange("h p d -> p h d")).then_inc(ctx_loaded, 16)
                        dma(vctx[:], cache_v[0, 0].rearrange("h p d -> p h d")).then_inc(ctx_loaded, 16)
                        sp.wait_ge(pad_loaded, 16)
                        rep = padsb[:, :]
                        dma(biasd[:], bass.AP(rep.tensor, rep.offset, [rep.ap[0], [0, GRID_W], [1, PADW]])).then_inc(rep_stored, 16)
                        n = ph["nout"]
                        sp.wait_ge(w_lo_ok, n - 1)
                        dma(raw[:, n % 2, 0:4, :].rearrange("p a b -> p (a b)"), ab_w_out[0][0:P, 0:512]).then_inc(w_loaded[n % 2], 16)
                        sp.wait_ge(in_evac[(nb + AB_UNITS) % 2], ph["iv_end"][(nb + AB_UNITS) % 2])
                        for kd in range(4):
                            dma(grow[:, kd, :], graw[kd * MLH:(kd + 1) * MLH, :]).then_inc(g_moved, 16)
                        dma(mprev[:, 0, 0:1], state_m[0, 0, 0].rearrange("(h a) -> h a", a=1), **slow).then_inc(m0_loaded, 16)
                        dma(mprev[:, 1, CT - 1:CT], state_m[0, 0, 1].rearrange("(h a) -> h a", a=1), **slow).then_inc(m0_loaded, 16)
                        sp.wait_ge(kv_out, 1)
                        dma(new_k[0, 0].rearrange("h p d -> p h d"), Sb[:, 0, 0:4, :].rearrange("p a b -> p (a b)").rearrange("p (h d) -> p h d", d=NAD)).then_inc(kv_done, 16)
                        dma(new_v[0, 0].rearrange("h p d -> p h d"), va[:, CT, :].rearrange("p (h d) -> p h d", d=NAD)).then_inc(kv_done, 16)
                        sp.wait_ge(rep_stored, 16)
                        sp.wait_ge(pe_unit, nb + AB_UNITS + 1)
                        for h in range(NAH):
                            if h >= 2:
                                sp.wait_ge(na_nm, NT * (h - 1))
                            for up in range(2):
                                row = h * DR + 1 - up
                                src = bass.AP(biasd.tensor, row * GRID_W * PADW + GRID_W - 1, [[PADW - 1, GRID_W], [GRID_W * PADW, TJ], [1, GRID_W]])
                                dma(T2[up * GRID_W:(up + 1) * GRID_W, h % 2], src).then_inc(bias_loaded[h % 2], 16)
                        sp.wait_ge(r_m, 1)
                        dma(new_m[0, 0, 0].rearrange("(h a) -> h a", a=1), mrw[:, 0, TOK - 1:TOK], **slow).then_inc(st_out, 16)
                        dma(new_m[0, 0, 1].rearrange("(h a) -> h a", a=1), mrw[:, 1, LAT:LAT + 1], **slow).then_inc(st_out, 16)
                        sp.wait_ge(aT_evac, 8)
                        for dr in range(2):
                            dma(Cs[:, dr, :, 0:MLD], state_C[0, 0, dr].rearrange("h p e -> p h e")).then_inc(st_loaded, 16)
                            dma(Cs[:, dr, :, MLD:MLD + 1], state_n[0, 0, dr].rearrange("h (p a) -> p h a", a=1), **slow).then_inc(st_loaded, 16)
                        for dr in range(2):
                            sp.wait_ge(ml_cs, 7 + dr)
                            dma(new_C[0, 0, dr].rearrange("h p e -> p h e"), Cs[:, dr, :, 0:MLD]).then_inc(st_out, 16)
                            dma(new_n[0, 0, dr].rearrange("h (p a) -> p h a", a=1), Cs[:, dr, :, MLD:MLD + 1], **slow).then_inc(st_out, 16)
                        sp.wait_ge(st_out, 16 * 6)
                        load_gate(s)
                        load_cols(s + 1)
                        for n2 in range(1, AB_OUT):
                            d, k = n2 // KD, n2 % KD
                            n = ph["nout"] + n2
                            sp.wait_ge(w_lo_ok, n - 1)
                            dma(raw[:, n % 2, 0:4, :].rearrange("p a b -> p (a b)"), ab_w_out[0][k * P:(k + 1) * P, d * 512:(d + 1) * 512]).then_inc(w_loaded[n % 2], 16)
            for t in range(NT):
                sp.wait_ge(x_new, NT * len(SUBS) - NT + t + 1)
                dst = ys[:, t, :] if t < CT else yp[:, 0, :]
                dma(dst, X[:, t, :]).then_inc(y_stored, 16)
            sp.wait_ge(y_stored, 16 * NT)

        @block.tensor
        def _(pe):
            mm = nc.tensor.matmul

            pe.wait_ge(csil_ok, 1)
            for i in range(PRO):
                for k in range(KD):
                    if k % (KD // 2) == 0:
                        pe.wait_ge(first_loaded[i][k // (KD // 2)], 16)
                    last = mm(PS[0:2, i, :], csil[:, :, k], ada0[:, i, k, :], start=(k == 0), stop=(k == KD - 1))
                last.then_inc(first_mm, 1)
            pe.wait_ge(first_row, PRO)
            pe.wait_ge(s_ident, 16)
            for kind in range(2):
                for k in range(KD):
                    col = (kind * KD + k) * 2
                    last = nc.tensor.transpose(PS[:, 0, col:col + 2], flat(mrow0[:])[:, kind * D + k:(kind + 1) * D:KD], ident[0:2, 0:2])
            last.then_inc(first_mm, 1)

            def sum_job(ph, q, i=0):
                j = ph["jb"] + q
                pe.wait_ge(ada_used[1], i + (j + 1))
                need(pe, mrow_ok, i + j)
                mm(PS[0:1, MODSUM, :], ones[:], acc[:].rearrange("p a b -> p (a b)"), start=True, stop=True).then_inc(mod_sum, 1)

            def three(out, a_hi, a_lo, b_hi, b_lo, first, final):
                mm(out, a_hi, b_hi, start=first, stop=False)
                mm(out, a_hi, b_lo, start=False, stop=False)
                return mm(out, a_lo, b_hi, start=False, stop=final)

            def turn_x(s):
                if s == 0:
                    pe.wait_ge(s_x, 32)
                    pe.wait_ge(neg_ok, 2)
                for t in range(NT):
                    pe.wait_ge(diag_ok, NT * s + t + 1)
                    if s and t < 2:
                        pe.wait_ge(out_evac, plan[s][0]["oe"] - (0 if t else NT))
                    if t >= 2:
                        pe.wait_ge(hmod_ok, NT * s + t - 1)
                    for k in range(KD):
                        last = mm(TR[t % 2][:, k, :], X[:, t, k::KD], diag[:, t % 2, :], start=True, stop=True)
                    last.then_inc(xT_ok, 1)

            def unit_half(p, h, width=P):
                for k in range(KD):
                    hi, lo = w_hi[:, p, k, 0:width], w_lo[:, p, k, 0:width]
                    for a, b in ((hi, hT_hi), (hi, hT_lo), (lo, hT_hi)):
                        last = mm(IN[p][0:width, h, 0:HT], a, b[:, k, h * HT:(h + 1) * HT],
                                  start=(k == 0 and a is hi and b is hT_hi), stop=(k == KD - 1 and a is lo))
                return last

            def first_units(s, ph):
                pe.wait_ge(out_evac, ph["oe"])
                if s == 0:
                    pe.wait_ge(first_row, PRO)
                for h in range(2):
                    pe.wait_ge(hT_ready, NT * s + (HT * (h + 1) + P - 1) // P)
                    for r in range(2):
                        n = ph["nin"] + r
                        pe.wait_ge(w_lo_ok, n + 1)
                        need(pe, in_evac[n % 2], inv(ph, n) - 1)
                        last = unit_half(n % 2, h)
                        if h:
                            last.then_inc(pe_unit, 1)

            def in_unit(ph, r, i, per, width=P):
                n = ph["nin"] + r
                p = n % 2
                pe.wait_ge(w_lo_ok, n + 1 + i * per)
                need(pe, in_evac[p], inv(ph, n) - 1 + i * (per // 2))
                for k in range(KD):
                    hi, lo = w_hi[:, p, k, 0:width], w_lo[:, p, k, 0:width]
                    for a, b in ((hi, hT_hi), (hi, hT_lo), (lo, hT_hi)):
                        for h in range(2):
                            last = mm(IN[p][0:width, h, 0:HT], a, b[:, k, h * HT:(h + 1) * HT],
                                      start=(k == 0 and a is hi and b is hT_hi), stop=(k == KD - 1 and a is lo))
                last.then_inc(pe_unit, 1)

            def out_phase(ph, a_hi, a_lo):
                for d in range(2):
                    for k in range(ph["k"]):
                        n = ph["nout"] + d * ph["k"] + k
                        pe.wait_ge(w_lo_ok, n + 1)
                        if d == 0:
                            pe.wait_ge(act_ready, ph["ar"] + k + 1)
                            if k == 0:
                                pe.wait_ge(out_evac, ph["oe"])
                                if ph.get("jobs"):
                                    sum_job(ph, ph["jobs"] - 1)
                                    pe.wait_ge(mrow_ok, ph["jb"] + ph["jobs"])
                        elif k >= 3 and k % 3 == 0 and (k - 3) // 3 < ph.get("late", 0):
                            pe.wait_ge(out_evac, ph["oe"] + NT)
                            sum_job(ph, ph["jobs"] + (k - 3) // 3)
                        for t in range(NT):
                            if k == 0 and d == 0 and t == NT - 1:
                                pe.wait_ge(in_evac[0], ph["iv_end"][0])
                            if k == 0 and d == 1:
                                if t == 0:
                                    pe.wait_ge(in_evac[0], ph["iv_end"][0])
                                    pe.wait_ge(in_evac[1], ph["iv_end"][1])
                                if t >= 3:
                                    pe.wait_ge(out_evac, ph["oe"] + t - 2)
                            tok = slice(t * P, (t + 1) * P)
                            b_hi = w_hi[:, n % 2, 0:4, :].rearrange("p a b -> p (a b)")
                            b_lo = w_lo[:, n % 2, 0:4, :].rearrange("p a b -> p (a b)")
                            last = three(PS[:, OUT[d][t], :], a_hi[:, k, tok], a_lo[:, k, tok], b_hi, b_lo, k == 0, k == ph["k"] - 1)
                            if k == ph["k"] - 1 and t < NT - 1:
                                last.then_inc(out_ready, 1)
                        last.then_inc(pe_unit, 1)

            def mixing(ph):
                s_base = ph["nin"]
                tr = 0

                def group(r0, turned):
                    nonlocal tr
                    def body(i):
                        if r0 or not first(i):
                            in_unit(ph, r0, i, 2)
                            in_unit(ph, r0 + 1, i, 2)
                        if turned:
                            for r in range(2):
                                n = s_base + r0 + r
                                p = n % 2
                                pe.wait_ge(in_evac[p], inv(ph, n) + i)
                                need(pe, tr_evac, i * 2 + (tr + r - 1))
                                for t in range(NT):
                                    last = nc.tensor.transpose(PS[:, 4 + 2 * r + t // 4, (t % 4) * P:(t % 4 + 1) * P],
                                                               ftmp[:, p, t * P:(t + 1) * P], ident[:])
                                last.then_inc(tr_done, 1)

                    body(0)
                    with pe.Fori(1, 2) as i:
                        body(i)
                    if turned:
                        tr += 4

                group(0, False)
                group(4, False)
                group(8, True)
                group(12, False)
                group(16, True)
                group(20, True)
                group(24, False)
                in_unit(ph, AB_UNITS, 0, 2, NG)
                pe.wait_ge(ctx_loaded, 32)
                pe.wait_ge(tr_evac, tr)
                for a in range(4):
                    last = nc.tensor.transpose(PS[:, 4, a * P:(a + 1) * P], ktok[:, 2 * a:2 * a + 2, :].rearrange("p a b -> p (a b)"), ident[:])
                last.then_inc(kc_done, 1)
                for a in range(4):
                    last = nc.tensor.transpose(PS[:, 5, a * P:(a + 1) * P], FT[:, 4 + a, LAT:TOK], ident[:])
                last.then_inc(kc_done, 1)
                pe.wait_ge(kc_evac, 2)
                pe.wait_ge(in_evac[0], ph["iv_end"][0])
                pe.wait_ge(in_evac[1], ph["iv_end"][1])

                def scores(i):
                    h, t = NA_ITEMS[i]
                    pp = slice((h % 2) * NAD, (h % 2 + 1) * NAD)
                    if i >= 2:
                        pe.wait_ge(na_p, i - 1)
                    q = FT[pp, h // 2, t * P:(t + 1) * P]
                    b = 2 * (i % 2)
                    if t < CT:
                        mm(PS[:, b, :], q, FT[pp, 4 + h // 2, 0:LAT], start=True, stop=True)
                        last = mm(PS[:, b + 1, 0:P], q, kcT[pp, h // 2, :], start=True, stop=True)
                    else:
                        last = mm(PS[:, b + 1, 0:P], q, FT[pp, 4 + h // 2, LAT:TOK], start=True, stop=True)
                    last.then_inc(na_s, 1)

                def turn(i):
                    h, t = NA_ITEMS[i]
                    pe.wait_ge(na_p, i + 1)
                    if i:
                        pe.wait_ge(na_pt, i)
                    for a in (range(NT) if t < CT else [CT]):
                        last = nc.tensor.transpose(PS[:, 4 + a // 4, (a % 4) * P:(a % 4 + 1) * P], Sb[:, i % 2, a, :], ident[:])
                    last.then_inc(na_t, 1)

                def weigh(i):
                    h, t = NA_ITEMS[i]
                    pe.wait_ge(na_pt, i + 1)
                    if i >= 2:
                        pe.wait_ge(na_ok, i - 1)
                    tiles = range(NT) if t < CT else [CT]
                    for a in tiles:
                        v = va[:, a, h * NAD:(h + 1) * NAD] if t == CT or a < CT else vctx[:, h, :]
                        last = mm(PS[:, 6 + i % 2, 0:NAD], PT[:, i % 2, a, :], v, start=(a == tiles[0]), stop=(a == CT))
                    last.then_inc(na_o, 1)

                NI = len(NA_ITEMS)
                for i in range(NI + 2):
                    if i < NI:
                        scores(i)
                    if 1 <= i <= NI:
                        turn(i - 1)
                    if i >= 2:
                        weigh(i - 2)
                pe.wait_ge(r_em, 1)
                pe.wait_ge(r_mp, 1)
                for qn, rows in enumerate((grow[:, 0::2, :], emrow)):
                    for dr in range(2):
                        for cc in range(NT):
                            col = ((qn * 2 + dr) * NT + cc) * MLH
                            nc.tensor.transpose(PS[:, 4, col:col + MLH], rows[:, dr, cc * P:(cc + 1) * P], ident[0:MLH, 0:MLH])
                pe.wait_ge(s_const, 48)
                for h in range(MLH):
                    last = mm(PS[:, 5, h * 2 * NT:(h + 1) * 2 * NT], sel[:, h, :], mprev[:].rearrange("p a b -> p (a b)"), start=True, stop=True)
                last.then_inc(col_done, 1)
                pe.wait_ge(na_ok, NI)
                for k in range(4):
                    if k >= 2:
                        pe.wait_ge(aT_evac, 2 * (k - 1))
                    for t in range(NT):
                        last = nc.tensor.transpose(PS[:, 2 * (k % 2) + t // 4, (t % 4) * P:(t % 4 + 1) * P], atok[:, t, k * P:(k + 1) * P], ident[:])
                    last.then_inc(aT_done, 1)


                def front(q):
                    dr, cc = ML_STEPS[q]
                    if q < 2:
                        pe.wait_ge(aT_evac, 8)
                    else:
                        pe.wait_ge(ml_x, q - 1)
                        pe.wait_ge(ml_wi, q - 1)
                    for h in range(MLH):
                        last = mm(PS[:, q % 2, h * P:(h + 1) * P], sel[:, h, :], Mrow[:, dr, cc * P:(cc + 1) * P], start=True, stop=True)
                    last.then_inc(ml_rm, 1)
                    if q >= 2:
                        pe.wait_ge(ml_st, q - 1)
                    for h in range(MLH):
                        last = mm(PS[:, 2 + q % 2, h * P:(h + 1) * P], FT[:, 12 + h, cc * P:(cc + 1) * P], FT[:, 8 + h, cc * P:(cc + 1) * P], start=True, stop=True)
                    last.then_inc(ml_qk, 1)

                def back(q):
                    dr, cc = ML_STEPS[q]
                    inter = cc < CT
                    pe.wait_ge(ml_st, q + 1)
                    pe.wait_ge(ml_qs, min(q + 1, 8))
                    if q:
                        pe.wait_ge(ml_h, q)
                    else:
                        pe.wait_ge(col_ok, 1)
                        pe.wait_ge(st_loaded, 64)
                        pe.wait_ge(ones_ok, 1)
                    if q >= 2 and inter:
                        pe.wait_ge(ml_cs, q - 1)
                    for h in range(MLH):
                        o_ = PS[:, 4 + h // 2, (h % 2) * 256:(h % 2) * 256 + MLD + 1]
                        last = mm(o_, STs[:, q % 2, h, :], vmt[:, cc, h, :], start=True, stop=not inter)
                        if inter:
                            last = mm(o_, qs[:, q % 2, h, :], Cs[:, dr, h, :], start=False, stop=True)
                    last.then_inc(ml_num, 1)
                    if q in NEEDS_STATE:
                        j = NEEDS_STATE.index(q)
                        pe.wait_ge(ml_vw, j + 1)
                        if j:
                            pe.wait_ge(ml_cs, j)
                        for h in range(MLH):
                            last = mm(PS[:, 6 + h // 2, (h % 2) * 256:(h % 2) * 256 + MLD + 1], kmt[:, cc, h, :], vw[:, j % 2, h, :], start=True, stop=True)
                        last.then_inc(ml_c, 1)

                for q in range(len(ML_STEPS) + 1):
                    if q < len(ML_STEPS):
                        front(q)
                    if q:
                        back(q - 1)
                pe.wait_ge(h_n_ok, NT)
                for h in range(MLH):
                    if h >= 2:
                        pe.wait_ge(hT2_evac, h - 1)
                    for t in range(NT):
                        last = nc.tensor.transpose(PS[:, 2 * (h % 2) + t // 4, (t % 4) * P:(t % 4 + 1) * P], hsum[:, t, h, :], ident[:])
                    last.then_inc(hT2_done, 1)

            for s, kind in enumerate(SUBS):
                turn_x(s)
                first_units(s, plan[s][0])
                for z, ph in enumerate(plan[s]):
                    if kind == "ffn":
                        if z:
                            for r in range(2):
                                pe.wait_ge(out_evac, ph["oe"] - NT + (3 if (ph["nin"] + r) % 2 else 1))
                                in_unit(ph, r, 0, 2)
                        with pe.Fori(1, HF) as i:
                            if ph["jobs"]:
                                sum_job(ph, -1, i)
                            in_unit(ph, 0, i, 2)
                            in_unit(ph, 1, i, 2)
                        out_phase(ph, act_hi, act_lo)
                    elif kind == "sc":
                        for r in range(2, 6):
                            in_unit(ph, r, 0, 6)
                        with pe.Fori(1, KD // 2) as i:
                            for r in range(6):
                                in_unit(ph, r, i, 6)
                        out_phase(ph, act_hi, act_lo)
                    else:
                        mixing(ph)
                        out_phase(ph, hT_hi, hT_lo)

        @block.scalar
        def _(act):
            A = nc.scalar.activation
            act.wait_ge(s_c, 32)
            A(csil[:], ccol[:], ACT.Silu).then_inc(csil_ok, 1)
            def split(n, i=0, per=0, shape=None):
                act.wait_ge(w_loaded[n % 2], (n // 2 + 1 + i * (per // 2)) * 16)
                need(act, pe_unit, n - 1 + i * per)
                src, dst = raw[:, n % 2], w_hi[:, n % 2]
                if shape == "out":
                    src, dst = src[:, 0:4, :], dst[:, 0:4, :]
                elif shape == "gates":
                    src, dst = src[:, :, 0:NG], dst[:, :, 0:NG]
                A(dst, src, ACT.Copy).then_inc(w_hi_ok, 1)

            def square_out(s, d, t):
                ph = plan[s][-1]
                act.wait_ge(out_evac, ph["oe"] + d * NT + t + 1)
                done = (ssq_half, ssq_post)[d]
                if d:
                    act.wait_ge(*((ssq_post, NT * s + t) if t else (ssq_half, NT * (s + 1))))
                elif t:
                    act.wait_ge(ssq_half, NT * s + t)
                A(junk[:, 0:512], part[:, t, d * 512:(d + 1) * 512], ACT.Square, scale=D ** -0.5,
                  accum_out=ssq[:, d, t:t + 1]).then_inc(done, 1)

            def square_x(s, t):
                if s == 0:
                    act.wait_ge(s_x, 32)
                    if t:
                        act.wait_ge(ssq_pre, t)
                else:
                    act.wait_ge(x_new, NT * (s - 1) + t + 1)
                A(part[:, t, :] if s else junk[:], X[:, t, :], ACT.Square, scale=D ** -0.5, accum_out=ssq[:, 2, t:t + 1]).then_inc(ssq_pre, 1)

            def modulate(s, t):
                act.wait_ge(xT_ok, NT * s + t + 1)
                if t == 0:
                    act.wait_ge(cols_ready, s + 1)
                if t >= 2:
                    act.wait_ge(hT_ready, NT * s + t - 1)
                for k in range(KD):
                    last = A(h_mod[:, t % 2, k, :], TR[t % 2][:, k, :], ACT.Identity,
                             scale=mcol[:, s % 2, 1, cond(t), k:k + 1], bias=mcol[:, s % 2, 0, cond(t), k:k + 1])
                last.then_inc(hmod_ok, 1)

            def boundary(s):
                for q in range(NT + 3):
                    if s and q < NT:
                        square_out(s - 1, 1, q)
                    if 1 <= q <= NT and s < len(SUBS):
                        square_x(s, q - 1)
                    if q >= 3 and s < len(SUBS):
                        modulate(s, q - 3)
                        if q == 6:
                            split(plan[s][0]["nin"] + 1)

            def out_splits(s, ph, nxt, final):
                total = 2 * ph["k"]
                for u in range(1, total):
                    split(ph["nout"] + u, shape="out")
                    if final and u >= ph["k"] + 2 and u - ph["k"] - 2 < NT:
                        square_out(s, 0, u - ph["k"] - 2)
                if nxt:
                    split(ph["nout"] + total)

            def ffn_in(ph):
                nb = ph["nin"]
                ffn_pair(ph, nb, 0, False)
                with act.Fori(1, HF - 1) as i:
                    ffn_pair(ph, nb, i, False)
                ffn_pair(ph, nb, HF - 1, True)

            def ffn_pair(ph, nb, i, last):
                if not (first(i) and ph["half"] == 0):
                    split(nb + 1, i, 2)
                act.wait_ge(pe_unit, nb + 1 + i * 2)
                need(act, in_evac[(nb + 1) % 2], inv(ph, nb + 1) - 1 + i)
                A(halves(sg[:]), IN_V[nb % 2], ACT.Silu).then_inc(in_evac[nb % 2], 1)
                split(nb + 2, i, 2, shape="out" if last else None)

            def sc_in(ph):
                nb = ph["nin"]

                def body(i, last):
                    for r in range(6):
                        fin = last and r == 5
                        if not (first(i) and r == 0):
                            split(nb + r + 1, i, 6, shape="out" if fin else None)
                        if r % 3 == 0:
                            act.wait_ge(pe_unit, nb + r + 1 + i * 6)
                            if r == 0:
                                act.wait_ge(act_ready, ph["ar"] + i * 2)
                            else:
                                act.wait_ge(act_ready, ph["ar"] + 1 + i * 2)
                            A(halves(sg[:]), IN_V[(nb + r) % 2], ACT.Copy).then_inc(in_evac[(nb + r) % 2], 1)

                body(0, False)
                with act.Fori(1, KD // 2 - 1) as i:
                    body(i, False)
                body(KD // 2 - 1, True)

            def mixing(ph):
                nb = ph["nin"]
                tr = 0

                def group(r0, dst, scale=None, func=ACT.Copy, turned=False):
                    nonlocal tr

                    def body(i):
                        for r in range(2):
                            n = nb + r0 + r
                            p = n % 2
                            if not (r0 == 0 and r == 0 and first(i)):
                                split(n + 1, i, 2)
                            act.wait_ge(pe_unit, n + 1 + i * 2)
                            kw = {} if scale is None else {"scale": scale}
                            if turned:
                                need(act, tr_done, i * 2 + (tr + r - 1))
                                a = A(halves(ftmp[:, p, :]), IN_V[p], func, **kw)
                            if dst is not None:
                                a = A(FT[:, bass.ds(i * 2 + dst + r, 1), :].rearrange("p a (b c) -> p (a b) c", b=2), IN_V[p], func, **kw)
                            a.then_inc(in_evac[p], 1)

                    body(0)
                    with act.Fori(1, 2) as i:
                        body(i)
                    if turned:
                        tr += 4

                group(0, 0, scale=NAD ** -0.5)
                group(4, 4)
                group(8, None, turned=True)
                group(12, 8)
                group(16, 12, scale=MLD ** -0.5, turned=True)
                group(20, None, turned=True)
                for r in range(4):
                    n = nb + 24 + r
                    split(n + 1, shape="gates" if r == 3 else None)
                    act.wait_ge(pe_unit, n + 1)
                    A(FT[:, 16 + r, :].rearrange("p (b c) -> p b c", b=2), IN_V[n % 2], ACT.Sigmoid).then_inc(in_evac[n % 2], 1)
                n = nb + AB_UNITS
                split(n + 1, shape="out")
                act.wait_ge(pe_unit, n + 1)
                A(halves(graw[:]), IN_V[n % 2][0:NG], ACT.Copy).then_inc(in_evac[n % 2], 1)
                act.wait_ge(kc_done, 1)
                A(kcT[:].rearrange("p a b -> p (a b)"), PS[:, 4, :], ACT.Copy).then_inc(kc_evac, 1)
                act.wait_ge(g_rows, 1)
                fg = grow[:, 1::2, :]
                A(mrw[:], fg, ACT.Abs).then_inc(r_abs, 1)
                act.wait_ge(r_abs, 1)
                A(mrw[:], mrw[:], ACT.Exp, scale=-1.0).then_inc(r_exp, 1)
                act.wait_ge(r_exp, 1)
                A(mrw[:], mrw[:], ACT.Ln, bias=1.0).then_inc(r_ln, 1)
                for i, (h, t) in enumerate(NA_ITEMS):
                    act.wait_ge(na_nm, i + 1)
                    if i >= 2:
                        act.wait_ge(na_t, i - 1)
                    nm = small[:, 4 * (i % 2) + 2:4 * (i % 2) + 3]
                    dd = small[:, 8 + 2 * (i % 4):8 + 2 * (i % 4) + 2]
                    if i >= 4:
                        act.wait_ge(na_ok, i - 3)
                    if t < CT:
                        p_loc = Sb[:, i % 2, 0:4, :].rearrange("p a b -> p (a b)")
                        A(p_loc, p_loc, ACT.Exp, bias=nm, accum_out=dd[:, 0:1])
                    A(Sb[:, i % 2, CT, :], PS[:, 2 * (i % 2) + 1, 0:P], ACT.Exp, bias=nm, accum_out=dd[:, 1:2]).then_inc(na_p, 1)
                act.wait_ge(na_o, len(NA_ITEMS))
                act.wait_ge(r_m, 1)
                A(emrow[:], mrw[:], ACT.Exp, scale=-1.0).then_inc(r_em, 1)
                for q, (dr, cc) in enumerate(ML_STEPS):
                    act.wait_ge(ml_x, q + 1)
                    if q == 0:
                        act.wait_ge(col_ok, 1)
                    if q >= 2:
                        act.wait_ge(ml_h, q - 1)
                        act.wait_ge(ml_qs, min(q - 1, 8))
                        act.wait_ge(ml_vw, sum(1 for z in NEEDS_STATE if z < q - 1))
                        act.wait_ge(ml_cs, sum(1 for z in NEEDS_STATE if z < q - 1))
                    for h in range(MLH):
                        last = A(wi[:, q % 2, h, :], PS[:, q % 2, h * P:(h + 1) * P], ACT.Exp, scale=-1.0, bias=mpb[:, h, dr, cc:cc + 1])
                    last.then_inc(ml_wi, 1)
                    A(Wx[:, q % 2], Wx[:, q % 2], ACT.Exp, scale=-1.0).then_inc(ml_w, 1)

            split(0)
            for s, kind in enumerate(SUBS):
                boundary(s)
                for ph in plan[s]:
                    if kind == "ffn":
                        ffn_in(ph)
                    elif kind == "sc":
                        sc_in(ph)
                    else:
                        mixing(ph)
                    final = ph is plan[s][-1]
                    out_splits(s, ph, not (s == len(SUBS) - 1 and final), final)
            boundary(len(SUBS))

        @block.gpsimd
        def _(pool):
            own = Steps(pool, s_pool)
            pool.memset(halfneg[:], -0.5).then_inc(neg_ok, 1)
            pool.memset(ones[:], 1.0).then_inc(neg_ok, 1)
            pool.wait_ge(neg_ok, 2)
            pool.wait_ge(s_ident, 16)

            def rsqrt(dst, tmp, src, width, scale):
                own.link(pool.tensor_scalar(tmp, src, scale, EPS, ALU.mult, ALU.add))
                return pool.tensor_tensor(dst, tmp, halfneg[:, 0:width], ALU.pow)

            def gate_first_half(s, t):
                pool.wait_ge(ssq_half, NT * s + t + 1)
                if t == 0:
                    pool.wait_ge(gate_ready, s + 1)
                if s:
                    pool.wait_ge(r_post, NT * s)
                pool.tensor_scalar(msq[:, 0, t:t + 1], ssq[:, 0, t:t + 1], EPS, None, ALU.add)
                pool.tensor_tensor(part[:, t, 0:512], part[:, t, 0:512], G[:, cond(t), 0:512], ALU.mult).then_inc(gated_half, 1)

            def post_r(s, t):
                pool.wait_ge(ssq_post, NT * s + t + 1)
                pool.wait_ge(gated_half, NT * (s + 1))
                own.link(pool.tensor_tensor(msq[:, 1, t:t + 1], ssq[:, 1, t:t + 1], msq[:, 0, t:t + 1], ALU.add))
                pool.tensor_tensor(rms[:, 1, t:t + 1], msq[:, 1, t:t + 1], halfneg[:, 0:1], ALU.pow).then_inc(r_post, 1)

            def pre_r(s, t):
                pool.wait_ge(ssq_pre, NT * s + t + 1)
                own.link(rsqrt(rms[:, 0, t:t + 1], msq[:, 2, t:t + 1], ssq[:, 2, t:t + 1], 1, 1.0))
                if t >= 2:
                    pool.wait_ge(xT_ok, NT * s + t - 1)
                pool.tensor_scalar(diag[:, t % 2, :], ident[:], rms[:, 0, t:t + 1], None, ALU.mult).then_inc(diag_ok, 1)

            for s, kind in enumerate(SUBS):
                for q in range(NT + 1):
                    if s and q < NT:
                        post_r(s - 1, q)
                    if q:
                        pre_r(s, q - 1)
                if kind == "sc":
                    pool.wait_ge(hT_ready, NT * (s + 1))
                    pool.memset(upad[:], 0.0).then_inc(conv_zero, 1)
                if kind == "ab":
                    pool.wait_ge(hT_ready, NT * (s + 1))
                    pool.memset(padsb[:], 0.0).then_inc(pad_zero, 1)
                    pool.memset(vmt[:, :, :, MLD:MLD + 1], 1.0).then_inc(ones_ok, 1)
                    pool.wait_ge(ones_ok, 1)
                    nv, nd = 0, 0
                    whole = [z[1] for q, z in enumerate(ML_STEPS) if z[1] in [y[1] for y in ML_STEPS[:q]]]

                    def head_r(n):
                        pool.wait_ge(h_ssq_ok, n + 1)
                        c4 = slice(whole[n] * MLH, (whole[n] + 1) * MLH)
                        rsqrt(hr[:, c4], hms[:, c4], hssq[:, c4], MLH, 1.0 / MLD).then_inc(h_r_ok, 1)

                    for q, (dr, cc) in enumerate(ML_STEPS):
                        edge = P - 1 if dr == 0 else 0
                        if cc < CT:
                            pool.wait_ge(ml_wi, q + 1)
                            if q >= 2:
                                pool.wait_ge(ml_num, q - 1)
                            pool.tensor_tensor(qs[:, q % 2], FT[:, 8:12, cc * P:(cc + 1) * P], wi[:, q % 2], ALU.mult).then_inc(ml_qs, 1)
                        if q in NEEDS_STATE:
                            pool.wait_ge(ml_w, q + 1)
                            if nv >= 2:
                                pool.wait_ge(ml_c, nv - 1)
                            wl = Wx[:, q % 2, :, edge:edge + 1].to_broadcast([P, MLH, MLD + 1])
                            pool.tensor_tensor(vw[:, nv % 2], vmt[:, cc], wl, ALU.mult).then_inc(ml_vw, 1)
                            nv += 1
                        if cc in [z[1] for z in ML_STEPS[:q]]:
                            nd += 1
                            if nd >= 2:
                                head_r(nd - 2)
                    head_r(NT - 1)
                for t in range(NT):
                    gate_first_half(s, t)
            for t in range(NT):
                post_r(len(SUBS) - 1, t)

        @block.vector
        def _(dve):
            own = Steps(dve, s_dve)
            V = nc.vector
            dve.wait_ge(firstb_loaded, 16)
            for i in range(PRO):
                dve.wait_ge(first_mm, i + 1)
                V.tensor_tensor(mrow0[:, i, :], PS[0:2, i, :], adab0[:, i * MODW:(i + 1) * MODW], ALU.add).then_inc(first_row, 1)

            def job_half(ph, q, h, i=0):
                j = ph["jb"] + q
                dve.wait_ge(ada_loaded[h], (i + (j + 1)) * 16)
                if h == 0:
                    need(dve, mod_sum, i + j)
                else:
                    own.wait_back(0)
                for k in range(KD // 2):
                    for cd in range(2):
                        if k:
                            own.wait_back(1)
                        col = csil[:, cd, h * (KD // 2) + k:h * (KD // 2) + k + 1]
                        w = ada[:, h, k, :]
                        if h == 0 and k == 0:
                            ins = V.tensor_scalar(acc[:, cd, :], w, col, None, ALU.mult)
                        else:
                            ins = V.scalar_tensor_tensor(acc[:, cd, :], w, col, acc[:, cd, :], ALU.mult, ALU.add)
                        own.mark(ins)
                own.wait_back(0)
                dve.sem_inc(ada_used[h], 1)

            def job_row(ph, q, i=0):
                j = ph["jb"] + q
                dve.wait_ge(mod_sum, i + (j + 1))
                dve.wait_ge(bias_in, (i + (j + 1)) * 16)
                need(dve, mod_stored, (i + j) * 16)
                V.tensor_tensor(mrow[:], PS[0:1, MODSUM, :].rearrange("p (a b) -> p a b", a=2),
                                adab[:, None, :].to_broadcast([1, 2, JW]), ALU.add).then_inc(mrow_ok, 1)

            def split(n, i=0, per=0, shape=None):
                dve.wait_ge(w_hi_ok, n + 1 + i * per)
                a, b, d_ = raw[:, n % 2], w_hi[:, n % 2], w_lo[:, n % 2]
                if shape == "out":
                    a, b, d_ = (z[:, 0:4, :] for z in (a, b, d_))
                elif shape == "gates":
                    a, b, d_ = (z[:, :, 0:NG] for z in (a, b, d_))
                V.tensor_tensor(d_, a, b.bitcast(F32), ALU.subtract).then_inc(w_lo_ok, 1)

            def scale_cols(s):
                if s == 0:
                    dve.wait_ge(first_mm, PRO + 1)
                    own.link(V.tensor_copy(mcol[:, 0].rearrange("p a c k -> p a k c"), PS[:, 0, 0:4 * KD].rearrange("p (a k c) -> p a k c", a=2, c=2)))
                dve.wait_ge(cols_loaded, 16 + 48 * s)
                m = mcol[:, s % 2, 1]
                g = gpre[:, s % 2, None, :].to_broadcast([P, 2, KD])
                V.scalar_tensor_tensor(m, m, 1.0, g, ALU.add, ALU.mult).then_inc(cols_ready, 1)

            def gate_tile(s):
                dve.wait_ge(gate_loaded, 32 * (s + 1))
                w = 1.0 if s % 3 == 1 else 0.5
                V.scalar_tensor_tensor(G[:], G[:], w, gpost[:, None, :].to_broadcast([P, 2, D]), ALU.mult, ALU.mult).then_inc(gate_ready, 1)

            def gate_second_half(s, t):
                dve.wait_ge(ssq_post, NT * s + t + 1)
                own.link(V.tensor_tensor(part[:, t, 512:D], part[:, t, 512:D], G[:, cond(t), 512:D], ALU.mult))

            def add_out(s, t):
                dve.wait_ge(r_post, NT * s + t + 1)
                V.scalar_tensor_tensor(X[:, t, :], part[:, t, :], rms[:, 1, t:t + 1], X[:, t, :], ALU.mult, ALU.add).then_inc(x_new, 1)

            def split_h(s, t):
                tok = slice(t * P, (t + 1) * P)
                dve.wait_ge(hmod_ok, NT * s + t + 1)
                own.link(V.tensor_copy(hT_hi[:, :, tok], h_mod[:, t % 2]))
                V.tensor_tensor(hT_lo[:, :, tok], h_mod[:, t % 2], hT_hi[:, :, tok].bitcast(F32), ALU.subtract).then_inc(hT_ready, 1)

            def evac(ph, d, t):
                if t < NT - 1:
                    dve.wait_ge(out_ready, OR(ph, d, t))
                else:
                    dve.wait_ge(pe_unit, ph["nout"] + (d + 1) * ph["k"])
                dst = part[:, t, d * 512:(d + 1) * 512]
                src = PS[:, OUT[d][t], :]
                if ph.get("half") == 1:
                    V.tensor_tensor(dst, src, dst, ALU.add).then_inc(out_evac, 1)
                else:
                    V.tensor_copy(dst, src).then_inc(out_evac, 1)

            def boundary(s):
                for q in range(NT + 4):
                    if s and q < NT:
                        evac(plan[s - 1][-1], 1, q)
                    if s and 1 <= q <= NT:
                        gate_second_half(s - 1, q - 1)
                        add_out(s - 1, q - 1)
                    if q >= 4 and s < len(SUBS):
                        split_h(s, q - 4)
                        if q == 7:
                            split(plan[s][0]["nin"] + 1)

            def out_phase(s, ph, nxt):
                K, jobs, late = ph["k"], ph.get("jobs", 0), ph.get("late", 0)
                assert K + 1 + 3 * late < 2 * K or not late
                final = ph is plan[s][-1]
                if jobs:
                    job_row(ph, jobs - 1)
                for u in range(1, 2 * K):
                    split(ph["nout"] + u, shape="out")
                    if u == K:
                        for t in range(NT):
                            evac(ph, 0, t)
                        if final:
                            gate_tile(s)
                    z, r = divmod(u - K - 1, 3)
                    if r == 0 and 0 < z <= late:
                        job_row(ph, jobs + z - 1)
                    if r < 2 and 0 <= z < late:
                        job_half(ph, jobs + z, r)
                if final and s + 1 < len(SUBS):
                    scale_cols(s + 1)
                if nxt:
                    split(ph["nout"] + 2 * K)
                if not final:
                    for t in range(NT):
                        evac(ph, 1, t)

            def split_act(k, hi, lo, src, i=0):
                own.link(V.tensor_copy(hi, src))
                V.tensor_tensor(lo, src, hi.bitcast(F32), ALU.subtract).then_inc(act_ready, 1)

            def ffn_pair(ph, i, last):
                nb = ph["nin"]
                if not (first(i) and ph["half"] == 0):
                    split(nb + 1, i, 2)
                if ph["jobs"]:
                    if not (first(i)):
                        job_row(ph, -1, i)
                    job_half(ph, 0, 0, i)
                split(nb + 2, i, 2, shape="out" if last else None)
                if ph["jobs"]:
                    job_half(ph, 0, 1, i)
                dve.wait_ge(pe_unit, nb + 2 + i * 2)
                dve.wait_ge(in_evac[nb % 2], inv(ph, nb) + i)
                need(dve, act_ready, ph["ar"] + i)
                p = (nb + 1) % 2
                V.tensor_tensor(halves(ut[:]), IN_V[p], halves(sg[:]), ALU.mult).then_inc(in_evac[p], 1)
                dve.wait_ge(in_evac[p], inv(ph, nb + 1) + i)
                if isinstance(i, int):
                    hi, lo = act_hi[:, i, :], act_lo[:, i, :]
                    u = ut[:]
                else:
                    hi, lo, u = act_hi[:, bass.ds(i, 1), :], act_lo[:, bass.ds(i, 1), :], ut[:, None, :]
                split_act(i, hi, lo, u)

            def ffn_in(ph):
                ffn_pair(ph, 0, False)
                with own.loop(1, HF - 1, 1 + (2 * KD if ph["jobs"] else 0)) as i:
                    ffn_pair(ph, i, False)
                ffn_pair(ph, HF - 1, True)

            def sc_in(ph):
                nb = ph["nin"]
                dve.wait_ge(conv_zero, 1)
                dve.wait_ge(s_slow, 64)
                pieces = [(0, 0, 0, HT), (1, 0, HT, LAT), (1, LAT - HT, LAT, TOK)]

                def body(i, last):
                    for jj in range(2):
                        n = nb + 3 * jj
                        if not (first(i) and jj == 0):
                            split(n + 1, i, 6)
                        split(n + 2, i, 6)
                        dve.wait_ge(pe_unit, n + 2 + i * 6)
                        dve.wait_ge(in_evac[n % 2], inv(ph, n) + i * 3)
                        for z, (h, f0, t0, t1) in enumerate(pieces):
                            off = 1 if t0 < LAT else 2
                            ins = V.tensor_tensor(upad[:, t0 + off:t1 + off], IN_V[(n + 1) % 2][:, h, f0:f0 + t1 - t0], sg[:, t0:t1], ALU.mult)
                        ins.then_inc(in_evac[(n + 1) % 2], 1)
                        dve.wait_ge(in_evac[(n + 1) % 2], inv(ph, n + 1) + i * 3)
                        col = lambda ap: ap[:, bass.ds(i * 2 + jj, 1)]
                        own.link(V.tensor_scalar(yconv[:], upad[:, 1:TOK + 2], col(cw[:, 1, :]), col(cb[:, :]), ALU.mult, ALU.add))
                        own.link(V.scalar_tensor_tensor(yconv[:], upad[:, 0:TOK + 1], col(cw[:, 0, :]), yconv[:], ALU.mult, ALU.add))
                        own.link(V.scalar_tensor_tensor(yconv[:], upad[:, 2:TOK + 3], col(cw[:, 2, :]), yconv[:], ALU.mult, ALU.add))
                        split(n + 3, i, 6, shape="out" if last and jj == 1 else None)
                        dve.wait_ge(pe_unit, n + 3 + i * 6)
                        for z, (h, f0, t0, t1) in enumerate(pieces):
                            off = 0 if t0 < LAT else 1
                            ins = V.tensor_tensor(ut[:, t0:t1], IN_V[n % 2][:, h, f0:f0 + t1 - t0], yconv[:, t0 + off:t1 + off], ALU.mult)
                        ins.then_inc(in_evac[n % 2], 1)
                        dve.wait_ge(in_evac[n % 2], inv(ph, n + 2) + i * 3)
                        hi, lo = (z[:, bass.ds(i * 2 + jj, 1), :] for z in (act_hi, act_lo))
                        split_act(None, hi, lo, ut[:, None, :])
                        dve.wait_ge(act_ready, ph["ar"] + jj + 1 + i * 2)

                body(0, False)
                with own.loop(1, KD // 2 - 1, 8) as i:
                    body(i, False)
                body(KD // 2 - 1, True)

            def mixing(ph):
                nb = ph["nin"]
                tr = 0
                for g, dst in enumerate((None, None, "va", None, "km", "vm", None)):
                    def body(i):
                        for r in range(2):
                            if not (g == 0 and r == 0 and first(i)):
                                split(nb + 4 * g + r + 1, i, 2)
                        if dst:
                            for r in range(2):
                                dve.wait_ge(tr_done, tr + r + 1 + i * 2)
                                src = flat(pair(4 + 2 * r))[:, 0:TOK].rearrange("p (t e) -> p t e", e=P)
                                if dst == "va":
                                    o_ = va[:, :, bass.ds(i * (2 * P) + r * P, P)]
                                else:
                                    z = kmt if dst == "km" else vmt
                                    o_ = z[:, :, bass.ds(i * 2 + r, 1), 0:MLD].rearrange("p t a e -> p t (a e)")
                                V.tensor_copy(o_, src).then_inc(tr_evac, 1)

                    body(0)
                    if g < 6:
                        with dve.Fori(1, 2) as i:
                            body(i)
                    if dst:
                        tr += 4
                split(nb + 27)
                split(nb + 28, shape="gates")
                split(nb + 29, shape="out")
                dve.wait_ge(kc_done, 2)
                own.link(V.tensor_copy(Sb[:, 0, 0:4, :].rearrange("p a b -> p (a b)"), PS[:, 5, :]))
                dve.sem_inc(kc_evac, 1)
                dve.sem_inc(kv_out, 1)

                dve.wait_ge(s_const, 48)

                def masked(h):
                    dve.wait_ge(bias_loaded[h % 2], 32 * (h // 2 + 1))
                    own.link(V.tensor_tensor(T2[:, h % 2], T2[:, h % 2], namask[:, None, :].to_broadcast([P, TJ, GRID_W]), ALU.add))

                def maxima(i):
                    h, t = NA_ITEMS[i]
                    if t == 0:
                        masked(h)
                    dve.wait_ge(na_s, i + 1)
                    if i == 0:
                        dve.wait_ge(kv_done, 32)
                        dve.wait_ge(kv_out, 1)
                    if i >= 2:
                        dve.wait_ge(na_t, i - 1)
                        dve.wait_ge(na_p, i - 1)
                    m = small[:, 4 * (i % 2):4 * (i % 2) + 4]
                    ctx_s = PS[:, 2 * (i % 2) + 1, 0:P]
                    if t < CT:
                        off = (ROWS - 2 - 2 * t)
                        bias = T2[:, h % 2, off:off + ROWS, :].rearrange("p a b -> p (a b)")
                        V.tensor_tensor_reduce(Sb[:, i % 2, 0:4, :].rearrange("p a b -> p (a b)"), PS[:, 2 * (i % 2), :], bias, 1.0, -BIG * 10, ALU.add, ALU.max, m[:, 0:1])
                        own.link(V.tensor_reduce(m[:, 1:2], ctx_s, AX.X, ALU.max))
                        V.tensor_scalar(m[:, 2:3], m[:, 0:1], m[:, 1:2], -1.0, ALU.max, ALU.mult).then_inc(na_nm, 1)
                    else:
                        own.link(V.tensor_reduce(m[:, 1:2], ctx_s, AX.X, ALU.max))
                        V.tensor_scalar(m[:, 2:3], m[:, 1:2], -1.0, None, ALU.mult).then_inc(na_nm, 1)

                def evac_T(i):
                    h, t = NA_ITEMS[i]
                    dve.wait_ge(na_t, i + 1)
                    if i >= 2:
                        dve.wait_ge(na_o, i - 1)
                    if t < CT:
                        V.tensor_copy(PT[:, i % 2].rearrange("p a b -> p (a b)"), flat(pair(4))[:, 0:TOK]).then_inc(na_pt, 1)
                    else:
                        V.tensor_copy(PT[:, i % 2, CT, :], PS[:, 5, 0:P]).then_inc(na_pt, 1)

                def divide(i):
                    h, t = NA_ITEMS[i]
                    dd = small[:, 8 + 2 * (i % 4):8 + 2 * (i % 4) + 2]
                    dve.wait_ge(na_o, i + 1)
                    if t < CT:
                        own.link(V.tensor_tensor(dd[:, 0:1], dd[:, 0:1], dd[:, 1:2], ALU.add))
                        own.link(V.reciprocal(dd[:, 0:1], dd[:, 0:1]))
                    else:
                        own.link(V.reciprocal(dd[:, 0:1], dd[:, 1:2]))
                    V.tensor_scalar(atok[:, t, h * NAD:(h + 1) * NAD], PS[:, 6 + i % 2, 0:NAD], dd[:, 0:1], None, ALU.mult).then_inc(na_ok, 1)

                aT = lambda k: flat(pair(2 * (k % 2)))[:, 0:TOK]

                def turn_attention():
                    dve.wait_ge(col_done, 1)
                    dve.wait_ge(st_out, 32)
                    for k in range(4):
                        dve.wait_ge(aT_done, k + 1)
                        V.tensor_copy(hT_hi[:, k, :], aT(k)).then_inc(aT_evac, 1)
                        dve.wait_ge(aT_evac, 2 * k + 1)
                        V.tensor_tensor(hT_lo[:, k, :], aT(k), hT_hi[:, k, :].bitcast(F32), ALU.subtract).then_inc(aT_evac, 1)

                fg, ig = grow[:, 1::2, :], grow[:, 0::2, :]
                rev = lambda ap: ap[:, ::-1]
                way = lambda dr, ap: rev(ap) if dr else ap

                def gate_bias():
                    dve.wait_ge(g_moved, 64)
                    dve.wait_ge(s_slow, 64)
                    own.link(V.tensor_tensor(grow[:], grow[:], gateb[:, :, None].to_broadcast([MLH, 4, TOK]), ALU.add))
                    V.memset(mprev[:, :, CT:NT], 0.0).then_inc(g_rows, 1)

                def log_forget():
                    dve.wait_ge(r_ln, 1)
                    own.link(V.scalar_tensor_tensor(fg, fg, 0.0, mrw[:], ALU.min, ALU.subtract))

                def running_sum(dr):
                    for cc in range(NT):
                        f = way(dr, grow[:, 2 * dr + 1, cc * P:(cc + 1) * P])
                        own.mark(V.tensor_tensor_scan(way(dr, brow[:, dr, cc * P:(cc + 1) * P]), f, f, 0.0, ALU.add, ALU.min))

                def stabiliser(dr):
                    dve.wait_ge(m0_loaded, 32)
                    dve.wait_ge(g_rows, 1)
                    start = mprev[:, 0, 0:1] if dr == 0 else mprev[:, 1, CT - 1:CT]
                    for lo_, hi_, m0 in ((0, LAT, start), (LAT, TOK, 0.0)):
                        own.mark(V.tensor_tensor_scan(way(dr, mrw[:, dr, lo_:hi_]), way(dr, grow[:, 2 * dr + 1, lo_:hi_]), way(dr, grow[:, 2 * dr, lo_:hi_]), m0, ALU.add, ALU.max))

                def chunk_starts():
                    own.link(V.tensor_tensor(ig, ig, brow[:], ALU.subtract))
                    own.mark(V.tensor_copy(mprev[:, 0, 1:CT], mrw[:, 0, P - 1:LAT - P:P]))
                    own.link(V.tensor_copy(mprev[:, 1, 0:CT - 1], mrw[:, 1, P:LAT:P]))
                    dve.sem_inc(r_m, 1)

                def rows(i):
                    if i == 1:
                        log_forget()
                    if i in (2, 3):
                        running_sum(i - 2)
                    if i in (4, 5):
                        stabiliser(i - 4)
                    if i == 5:
                        own.wait_back(0)
                    if i == 6:
                        chunk_starts()

                gate_bias()
                NI = len(NA_ITEMS)
                for i in range(NI + 2):
                    rows(i)
                    if i < NI:
                        maxima(i)
                    if 1 <= i <= NI:
                        evac_T(i - 1)
                    if i >= 2:
                        divide(i - 2)
                V.tensor_tensor(Mrow[:], mrw[:], brow[:], ALU.subtract).then_inc(r_mp, 1)
                turn_attention()
                dve.wait_ge(col_done, 1)
                own.link(V.tensor_copy(ecol[:].rearrange("p a b c d -> p (a b c d)"), PS[:, 4, 0:4 * NT * MLH]))
                V.tensor_copy(mpb[:].rearrange("p a b c -> p (a b c)"), PS[:, 5, 0:2 * NT * MLH]).then_inc(col_ok, 1)

                seen = set()

                def decay(q):
                    dr, cc = ML_STEPS[q]
                    dve.wait_ge(ml_rm, q + 1)
                    if q >= 2:
                        dve.wait_ge(ml_st, q - 1)
                        dve.wait_ge(ml_vw, sum(1 for z in NEEDS_STATE if z < q - 1))
                    e = ecol[:, 0, dr, cc, :, None].to_broadcast([P, MLH, P])
                    rm = PS[:, q % 2, :].rearrange("p (h t) -> p h t", h=MLH)
                    own.link(V.tensor_tensor(Wx[:, q % 2], rm, e, ALU.subtract))
                    V.tensor_tensor(Wx[:, q % 2], Wx[:, q % 2], mlmask[:, dr, None, :].to_broadcast([P, MLH, P]), ALU.add).then_inc(ml_x, 1)

                def finish(q):
                    dr, cc = ML_STEPS[q]
                    edge = P - 1 if dr == 0 else 0
                    dve.wait_ge(ml_w, q + 1)
                    dve.wait_ge(ml_qk, q + 1)
                    if q >= 2:
                        dve.wait_ge(ml_num, q - 1)
                    V.tensor_tensor(STs[:, q % 2], PS[:, 2 + q % 2, :].rearrange("p (h t) -> p h t", h=MLH), Wx[:, q % 2], ALU.mult).then_inc(ml_st, 1)
                    dve.wait_ge(ml_num, q + 1)
                    num = pair(4).rearrange("p a (b c) -> p (a b) c", b=2)
                    dn = den[:, q % 2, :]
                    own.link(V.tensor_tensor(dn, num[:, :, MLD], ecol[:, 1, dr, cc, :], ALU.max))
                    own.link(V.scalar_tensor_tensor(dn, num[:, :, MLD], -1.0, dn, ALU.mult, ALU.max))
                    own.link(V.reciprocal(dn, dn))
                    r_ = den[:, q % 2, :, None].to_broadcast([P, MLH, MLD])
                    if cc in seen:
                        own.link(V.tensor_tensor(htmp[:], num[:, :, 0:MLD], r_, ALU.mult))
                        V.tensor_tensor(hsum[:, cc], hsum[:, cc], htmp[:], ALU.add).then_inc(ml_h, 1)
                    else:
                        seen.add(cc)
                        V.tensor_tensor(hsum[:, cc], num[:, :, 0:MLD], r_, ALU.mult).then_inc(ml_h, 1)
                    if q in NEEDS_STATE:
                        j = NEEDS_STATE.index(q)
                        dve.wait_ge(ml_c, j + 1)
                        dve.wait_ge(ml_wi, q + 1)
                        cu = pair(6).rearrange("p a (b c) -> p (a b) c", b=2)[:, :, 0:MLD + 1]
                        if cc < CT:
                            for h in range(MLH):
                                last = V.scalar_tensor_tensor(Cs[:, dr, h, :], Cs[:, dr, h, :], wi[:, q % 2, h, edge:edge + 1], cu[:, h, :], ALU.mult, ALU.add)
                        else:
                            last = V.tensor_copy(Cs[:, dr], cu)
                        last.then_inc(ml_cs, 1)

                whole = [cc for q, (dr, cc) in enumerate(ML_STEPS) if cc in [z[1] for z in ML_STEPS[:q]]]

                def head_square(n):
                    cc = whole[n]
                    own.link(V.tensor_tensor(htmp[:], hsum[:, cc], hsum[:, cc], ALU.mult))
                    V.tensor_reduce(hssq[:, cc * MLH:(cc + 1) * MLH], htmp[:], AX.X, ALU.add).then_inc(h_ssq_ok, 1)

                def head_scale(n):
                    cc = whole[n]
                    dve.wait_ge(h_r_ok, n + 1)
                    r_ = hr[:, cc * MLH:(cc + 1) * MLH, None].to_broadcast([P, MLH, MLD])
                    V.tensor_tensor(hsum[:, cc], hsum[:, cc], r_, ALU.mult).then_inc(h_n_ok, 1)

                decay(0)
                done = 0
                for q in range(len(ML_STEPS)):
                    if q + 1 < len(ML_STEPS):
                        decay(q + 1)
                    finish(q)
                    if ML_STEPS[q][1] in [z[1] for z in ML_STEPS[:q]]:
                        dve.wait_ge(ml_h, q + 1)
                        head_square(done)
                        if done:
                            head_scale(done - 1)
                        done += 1
                head_scale(4)
                dve.wait_ge(in_evac[0], ph["iv_end"][0])
                for h in range(MLH):
                    dve.wait_ge(hT2_done, h + 1)
                    V.scalar_tensor_tensor(ut[:], aT(h), hnorm[:, h:h + 1], FT[:, 16 + h, :], ALU.mult, ALU.mult).then_inc(hT2_evac, 1)
                    dve.wait_ge(hT2_evac, h + 1)
                    own.link(V.tensor_copy(hT_hi[:, 4 + h, :], ut[:]))
                    own.link(V.tensor_tensor(hT_lo[:, 4 + h, :], ut[:], hT_hi[:, 4 + h, :].bitcast(F32), ALU.subtract))
                dve.sem_inc(act_ready, KD)

            split(0)
            scale_cols(0)
            for s, kind in enumerate(SUBS):
                boundary(s)
                for ph in plan[s]:
                    if kind == "ffn":
                        ffn_in(ph)
                    elif kind == "sc":
                        sc_in(ph)
                    else:
                        mixing(ph)
                    out_phase(s, ph, not (s == len(SUBS) - 1 and ph is plan[s][-1]))
            boundary(len(SUBS))


NEEDS_STATE = [0, 1, 2, 3, 4, 5, 8, 9]

_INS = ['x_prompt', 'x_sample', 'cache_k', 'cache_v', 'state_C', 'state_n', 'state_m', 'c', 'c_ctx', 'ada_w',
        'ada_b', 'norm_g', 'ffn_w13', 'ffn_w2', 'ab_w_in', 'ab_w_out', 'na_rpb', 'ml_gate_b', 'ml_hnorm',
        'sc_w_in', 'sc_conv_w', 'sc_conv_b', 'sc_w_out']
_OUTS = [(1, 128, 1024), (1, 512, 1024), (1, 1, 8, 128, 64), (1, 1, 8, 128, 64), (1, 1, 2, 4, 128, 128),
         (1, 1, 2, 4, 128), (1, 1, 2, 4)]


def constants():
    import numpy as np
    ident = np.eye(P, dtype=np.float32)
    sel = np.zeros((MLH, MLH, P), np.float32)
    for h in range(MLH):
        sel[h, h, :] = 1.0
    s, t = np.arange(P)[:, None], np.arange(P)[None, :]
    mlmask = np.stack([np.where(s <= t, 0.0, BIG), np.where(s >= t, 0.0, BIG)], axis=1).astype(np.float32)
    q, k = np.arange(P)[:, None] % GRID_W, np.arange(GRID_W)[None, :]
    c0 = np.clip(q - WIN_W // 2, 0, GRID_W - WIN_W)
    namask = np.where((k >= c0) & (k < c0 + WIN_W), 0.0, -BIG).astype(np.float32)
    return {"k_ident": ident, "k_sel": sel, "k_mlmask": mlmask, "k_namask": namask}


def kernel(**inputs):
    import numpy as _np
    import concourse.bacc as _bacc
    from concourse import mybir as _mybir
    from concourse.bass_utils import run_bass_kernel_spmd as _run

    nc = _bacc.Bacc("TRN2", target_bir_lowering=False, num_devices=1)
    arrays, args = {}, []
    data = {name: _np.ascontiguousarray(inputs[name]) for name in _INS}
    data.update(constants())
    for name, a in data.items():
        arrays[f"in_{name}_dram"] = a
        args.append(nc.dram_tensor(f"in_{name}_dram", a.shape, _mybir.dt.from_np(a.dtype), kind="ExternalInput").ap())
    for i, shape in enumerate(_OUTS):
        args.append(nc.dram_tensor(f"out_{i}_dram", shape, _mybir.dt.float32, kind="ExternalOutput").ap())
    build(nc, *args)
    r = _run(nc, [arrays], core_ids=[0])
    return tuple(r.results[0][f"out_{i}_dram"] for i in range(len(_OUTS)))
```
